# Optimizing a Trainium2 kernel written in Bass

```python
import math
import jax, jax.numpy as jnp
from jax import lax
import numpy as np

D_MODEL = 1024
BATCH = 1
SEQ = 256
DEPTH = 4

N_MIXERS = 3
D_FF = 2816
CONV_WIDTH = 3
POOL_WINDOWS = (2, 4, 8, 16)
POOL_GROUPS = len(POOL_WINDOWS)
POOL_CH = D_MODEL // POOL_GROUPS
HEAD_DIM = 64
N_HEADS = D_MODEL // HEAD_DIM
N_KV_HEADS = 2
GQA_GROUP = N_HEADS // N_KV_HEADS
WINDOW = 128
BLOCK = 128
NUM_BUCKETS = 32
MAX_EXACT = NUM_BUCKETS // 2
MAX_DISTANCE = 128
EPS = 1e-6

N_A = (DEPTH + 2) // 3
N_B = (DEPTH + 1) // 3
N_C = DEPTH // 3

kernel_name = "interleaved_hybrid_conv_pool_swa_macaron"

def rmsnorm(x, g):
    xf = x.astype(jnp.float32)
    xf = xf * lax.rsqrt(jnp.mean(xf * xf, axis=-1, keepdims=True) + EPS)
    return (xf * g.astype(jnp.float32)).astype(x.dtype)

def swiglu(h, w_in, w_out):
    gate, up = jnp.split(h @ w_in, 2, axis=-1)
    return (jax.nn.silu(gate) * up) @ w_out

def short_conv_mixer(h, w_in, conv_w, w_out):
    b, c, v = jnp.split(h @ w_in, 3, axis=-1)
    z = c * v
    zp = jnp.pad(z, ((0, 0), (CONV_WIDTH - 1, 0), (0, 0)))
    s = z.shape[1]
    conv = conv_w[0] * zp[:, 0:s] + conv_w[1] * zp[:, 1:s + 1] + conv_w[2] * zp[:, 2:s + 2]
    return (b * conv) @ w_out

def multiscale_pool_mixer(h, w, bias, scale):
    bsz, s, d = h.shape
    hf = h.astype(jnp.float32).reshape(bsz, s, POOL_GROUPS, POOL_CH)
    cs = jnp.cumsum(hf, axis=1)
    t = jnp.arange(s)
    outs = []
    for g, win in enumerate(POOL_WINDOWS):
        c = cs[:, :, g]
        lower = jnp.pad(c, ((0, 0), (win, 0), (0, 0)))[:, :s]
        cnt = jnp.minimum(t + 1, win).astype(jnp.float32)[None, :, None]
        outs.append((c - lower) / cnt - hf[:, :, g])
    diff = jnp.stack(outs, axis=2).astype(h.dtype)
    y = jnp.einsum('bsgc,gcd->bsgd', diff, w).reshape(bsz, s, d) + bias
    return y * scale

def t5_causal_buckets(n):
    nf = np.maximum(n, 1).astype(np.float32)
    large = MAX_EXACT + (np.log(nf / MAX_EXACT) / math.log(MAX_DISTANCE / MAX_EXACT)
                         * (NUM_BUCKETS - MAX_EXACT)).astype(np.int32)
    large = np.minimum(large, NUM_BUCKETS - 1)
    return np.where(n < MAX_EXACT, n, large).astype(np.int32)

def head_rms(x, g):
    xf = x.astype(jnp.float32)
    xf = xf * lax.rsqrt(jnp.mean(xf * xf, axis=-1, keepdims=True) + EPS)
    return (xf * g.astype(jnp.float32)).astype(x.dtype)

def swa_attention_mixer(h, w_qkv, b_qkv, q_gain, k_gain, sinks, w_o, b_o, rel_bias):
    bsz, s, _ = h.shape
    nblk = s // BLOCK
    qkv = h @ w_qkv + b_qkv
    q, k, v = jnp.split(qkv, [N_HEADS * HEAD_DIM, (N_HEADS + N_KV_HEADS) * HEAD_DIM], axis=-1)
    q = head_rms(q.reshape(bsz, s, N_KV_HEADS, GQA_GROUP, HEAD_DIM), q_gain)
    k = head_rms(k.reshape(bsz, s, N_KV_HEADS, HEAD_DIM), k_gain)
    v = v.reshape(bsz, s, N_KV_HEADS, HEAD_DIM)

    q = q.reshape(bsz, nblk, BLOCK, N_KV_HEADS, GQA_GROUP, HEAD_DIM)

    def band(t):
        tb = t.reshape(bsz, nblk, BLOCK, N_KV_HEADS, HEAD_DIM)
        prev = jnp.concatenate([jnp.zeros_like(tb[:, :1]), tb[:, :-1]], axis=1)
        return jnp.concatenate([prev, tb], axis=2)

    kw, vw = band(k), band(v)
    scores = jnp.einsum('bnqhgd,bnkhd->bnhgqk', q, kw).astype(jnp.float32) * (HEAD_DIM ** -0.5)

    qi = np.arange(BLOCK)[:, None]
    ki = np.arange(2 * BLOCK)[None, :]
    dist = qi + BLOCK - ki
    buckets = t5_causal_buckets(dist)
    bias = rel_bias.astype(jnp.float32)[buckets]
    bias = jnp.transpose(bias, (2, 0, 1)).reshape(N_KV_HEADS, GQA_GROUP, BLOCK, 2 * BLOCK)
    scores = scores + bias[None, None]

    in_band = (dist >= 0) & (dist < WINDOW)
    key_pos = jnp.arange(nblk)[:, None, None] * BLOCK - BLOCK + jnp.asarray(ki)[None]
    mask = jnp.asarray(in_band)[None] & (key_pos >= 0)
    scores = jnp.where(mask[None, :, None, None], scores, -jnp.inf)

    sink = sinks.astype(jnp.float32).reshape(N_KV_HEADS, GQA_GROUP)[None, None, :, :, None, None]
    m = jnp.maximum(jnp.max(scores, axis=-1, keepdims=True), sink)
    p = jnp.exp(scores - m)
    denom = jnp.sum(p, axis=-1, keepdims=True) + jnp.exp(sink - m)
    probs = (p / denom).astype(vw.dtype)
    o = jnp.einsum('bnhgqk,bnkhd->bnqhgd', probs, vw).reshape(bsz, s, N_HEADS * HEAD_DIM)
    return o @ w_o + b_o

def setup_inputs(seed: int = 0) -> dict:
    key = jax.random.key(seed)
    ks = iter(jax.random.split(key, 32))

    def nrm(shape, scale):
        return jax.random.normal(next(ks), shape, jnp.float32) * scale

    def gain(shape):
        return 1.0 + nrm(shape, 0.1)

    qkv_w = (N_HEADS + 2 * N_KV_HEADS) * HEAD_DIM
    return {
        "x": nrm((BATCH, SEQ, D_MODEL), 1.0),
        "ffn1_norm": gain((DEPTH, D_MODEL)),
        "ffn1_w_in": nrm((DEPTH, D_MODEL, 2 * D_FF), D_MODEL ** -0.5),
        "ffn1_w_out": nrm((DEPTH, D_FF, D_MODEL), D_FF ** -0.5),
        "mix_norm": gain((DEPTH, D_MODEL)),
        "ffn2_norm": gain((DEPTH, D_MODEL)),
        "ffn2_w_in": nrm((DEPTH, D_MODEL, 2 * D_FF), D_MODEL ** -0.5),
        "ffn2_w_out": nrm((DEPTH, D_FF, D_MODEL), D_FF ** -0.5),
        "conv_w_in": nrm((N_A, D_MODEL, 3 * D_MODEL), D_MODEL ** -0.5),
        "conv_w": nrm((N_A, CONV_WIDTH, D_MODEL), CONV_WIDTH ** -0.5),
        "conv_w_out": nrm((N_A, D_MODEL, D_MODEL), D_MODEL ** -0.5),
        "pool_w": nrm((N_B, POOL_GROUPS, POOL_CH, POOL_CH), POOL_CH ** -0.5),
        "pool_b": nrm((N_B, D_MODEL), 0.02),
        "pool_scale": 0.5 + nrm((N_B, D_MODEL), 0.05),
        "attn_w_qkv": nrm((N_C, D_MODEL, qkv_w), D_MODEL ** -0.5),
        "attn_b_qkv": nrm((N_C, qkv_w), 0.02),
        "attn_q_norm": gain((N_C, HEAD_DIM)),
        "attn_k_norm": gain((N_C, HEAD_DIM)),
        "attn_sinks": nrm((N_C, N_HEADS), 0.5),
        "attn_w_o": nrm((N_C, N_HEADS * HEAD_DIM, D_MODEL), (N_HEADS * HEAD_DIM) ** -0.5),
        "attn_b_o": nrm((N_C, D_MODEL), 0.02),
        "rel_bias": nrm((NUM_BUCKETS, N_HEADS), 0.5),
    }

def reference(x, ffn1_norm, ffn1_w_in, ffn1_w_out, mix_norm, ffn2_norm, ffn2_w_in, ffn2_w_out,
              conv_w_in, conv_w, conv_w_out, pool_w, pool_b, pool_scale,
              attn_w_qkv, attn_b_qkv, attn_q_norm, attn_k_norm, attn_sinks, attn_w_o, attn_b_o,
              rel_bias):
    for i in range(DEPTH):
        x = x + 0.5 * swiglu(rmsnorm(x, ffn1_norm[i]), ffn1_w_in[i], ffn1_w_out[i])
        h = rmsnorm(x, mix_norm[i])
        kind, j = i % N_MIXERS, i // N_MIXERS
        if kind == 0:
            y = short_conv_mixer(h, conv_w_in[j], conv_w[j], conv_w_out[j])
        elif kind == 1:
            y = multiscale_pool_mixer(h, pool_w[j], pool_b[j], pool_scale[j])
        else:
            y = swa_attention_mixer(h, attn_w_qkv[j], attn_b_qkv[j], attn_q_norm[j], attn_k_norm[j],
                                    attn_sinks[j], attn_w_o[j], attn_b_o[j], rel_bias)
        x = x + y
        x = x + 0.5 * swiglu(rmsnorm(x, ffn2_norm[i]), ffn2_w_in[i], ffn2_w_out[i])
    return x


_drawn_inputs = setup_inputs


def setup_inputs(seed=0):
    import zlib

    import numpy as np

    out = dict(_drawn_inputs(seed))
    spreads = {}
    factors = {'pool_b': 5.934,
     'attn_b_qkv': 3.533,
     'attn_q_norm': 3.162,
     'attn_k_norm': 3.825,
     'attn_sinks': 25.051,
     'attn_b_o': 3.751}
    for name, (base, spread) in spreads.items():
        noise = np.random.default_rng([zlib.crc32(name.encode()), seed]).standard_normal(out[name].shape)
        drawn = base * np.exp(spread * noise) if base else spread * noise
        out[name] = __import__('jax').numpy.asarray(drawn.astype(out[name].dtype))
    for name, factor in factors.items():
        out[name] = (out[name] * factor).astype(out[name].dtype)
    return out
```

```python
from contextlib import ExitStack

import concourse.bass as bass
from concourse import mybir

F32 = mybir.dt.float32
F32R = mybir.dt.float32r
ALU = mybir.AluOpType
ACT = mybir.ActivationFunctionType
AX = mybir.AxisListType

P = 128
D = 1024
SEQ = 256
DEPTH = 4
DFF = 2816
HALVES = SEQ // P
KC = D // P
UNIT = 1024
RING = 6
FT = 256
FTILES = DFF // FT
IN_UNITS = KC * 2 * FT // UNIT
OUT_UNITS = 2
FFN_UNITS = FTILES * (IN_UNITS + OUT_UNITS)
CONV_TILES = 6
CV_TILES = 4
CONV_UNITS = CONV_TILES * IN_UNITS + KC
POOL_UNITS = 2
POOL_WINDOWS = (2, 4, 8, 16)
HEADS = 16
KV_HEADS = 2
HD = 64
QKV = (HEADS + 2 * KV_HEADS) * HD
NQK = HEADS + KV_HEADS
KV_UNITS = 2
ATTN_UNITS = 2 * IN_UNITS + KV_UNITS + KC
BAND = 384
EPS = 1e-6
TAPS = 3

FFN, CONV, POOL, ATTN = "ffn", "conv", "pool", "attn"
UNITS = {FFN: FFN_UNITS, CONV: CONV_UNITS, POOL: POOL_UNITS, ATTN: ATTN_UNITS}
INS = {FFN: 2 * FTILES, CONV: 2 * CONV_TILES, POOL: 0, ATTN: 2 * 3 + HEADS}
FILLS = {FFN: 2 * FTILES, CONV: 2 * CONV_TILES, POOL: 0, ATTN: 6 + 4 + 8 + 4}
ACCS = {FFN: 2, CONV: 2, POOL: 2, ATTN: 4}
NORM_FILLS = 4


class Phase:

    def __init__(self, kind, index, layer, before):
        self.kind, self.index, self.layer = kind, index, layer
        self.unit = before.unit + UNITS[before.kind] if before else 0
        self.into = before.into + INS[before.kind] if before else 0
        self.norm_fill = before.fill + FILLS[before.kind] if before else 0
        self.fill = self.norm_fill + NORM_FILLS
        self.acc = before.acc + ACCS[before.kind] if before else 0
        self.next_unit = self.unit + UNITS[kind]


def make_phases():
    phases = []
    for layer, mixer in enumerate((CONV, POOL, ATTN, CONV)):
        for kind in (FFN, mixer, FFN):
            phases.append(Phase(kind, len(phases), layer, phases[-1] if phases else None))
    return phases


def build(nc, stream, x_in, gains, taps, pool_b, pool_scale, b_qkv, q_gain, k_gain, sinks, b_o,
          rel_bias, ident_in, band_in, onehot_in, mask_in, table, spread, out):
    phases = make_phases()
    units_total = phases[-1].next_unit
    assert units_total % RING == 0 and all(p.into % 2 == 0 and p.fill % 2 == 0 for p in phases)

    ctx = ExitStack()
    with ctx:
        def sb(name, shape, dt=F32):
            return ctx.enter_context(nc.sbuf_tensor(name, shape, dt))

        def sem(name):
            return ctx.enter_context(nc.semaphore(name))

        raw = sb("raw", [P, RING, UNIT])
        w_hi = sb("w_hi", [P, RING, UNIT], F32R)
        w_lo = sb("w_lo", [P, RING, UNIT], F32R)
        x = sb("x", [P, HALVES, D])
        xn = sb("xn", [P, HALVES, D])
        h_hi = sb("h_hi", [P, HALVES, KC, P], F32R)
        h_lo = sb("h_lo", [P, HALVES, KC, P], F32R)
        u_hi = sb("u_hi", [P, HALVES, KC, P], F32R)
        u_lo = sb("u_lo", [P, HALVES, KC, P], F32R)
        gain = sb("gain", [P, 2, D])
        sumsq = sb("sumsq", [P, HALVES])
        meansq = sb("meansq", [P, HALVES])
        rstd = sb("rstd", [P, HALVES])
        neg_half = sb("neg_half", [P, NQK])
        gated = sb("gated", [P, HALVES, FT])
        act = sb("act", [P, HALVES, FT])
        ident = sb("ident", [P, P])
        MIX = 15616
        mix = sb("mix", [P, MIX])
        tap = sb("tap", [P, 2, TAPS, KC])

        def part(at, *shape):
            n = 1
            for s in shape:
                n *= s
            assert at + n <= MIX
            names = " ".join("abc"[:len(shape)])
            kw = {c: s for c, s in zip("abc", shape)}
            return mix[:, at:at + n].rearrange(f"p ({names}) -> p {names}", **kw), at + n

        z_t, a = part(0, KC, SEQ + TAPS - 1)
        conv, a = part(a, KC, SEQ)
        b_rows, a = part(a, HALVES, 512)
        gated_t, a = part(a, HALVES, 512)
        averaging, a = part(0, 4, 2, SEQ)
        pool_rows, a = part(a, 2, D)
        pool_y, a = part(a, HALVES, D)
        rel, a = part(0, HEADS, SEQ)
        bias_qkv, b = part(a, 1, QKV)
        qk_sq, b = part(b, 1, NQK * HD)
        scores, a = part(a, HEADS, SEQ)
        probs_t, a = part(a, 32, P)
        qkv, a = part(a, HALVES, QKV)
        k_twice, a = part(a, KV_HEADS, P)
        k_t, a = part(a, KV_HEADS, SEQ)
        q_t = probs_t[:, 16:32, :].rearrange("p (t c) k -> p t c k", t=HALVES)
        qk_gain = sb("qk_gain", [P, 2, HD])
        b_o_row = sb("b_o_row", [P, D])
        small = sb("small", [P, 12, NQK])
        rel_space, a = part(0, 3 * BAND + HEADS)
        onehot = rel_space[0:32, 0:BAND]
        rel_in = rel_space[0:32, 3 * BAND:3 * BAND + HEADS]
        mask_rows = rel_space[0:HEADS, BAND:2 * BAND]
        rel_rows = rel_space[0:HEADS, 2 * BAND:3 * BAND]

        into = [ctx.enter_context(nc.psum_tensor(f"into{i}", [P, 512], F32)) for i in range(2)]
        turn = [ctx.enter_context(nc.psum_tensor(f"turn{i}", [P, 512], F32)) for i in range(2)]
        accum = [ctx.enter_context(nc.psum_tensor(f"accum{i}", [P, D], F32)) for i in range(2)]

        raw_landed = [sem(f"raw_landed{s}") for s in range(RING)]
        hi_made = sem("hi_made")
        lo_made = sem("lo_made")
        unit_used = sem("unit_used")
        in_done = sem("in_done")
        gate_done = sem("gate_done")
        in_read = sem("in_read")
        turned = sem("turned")
        turn_hi = sem("turn_hi")
        turn_read = sem("turn_read")
        acc_done = sem("acc_done")
        acc_read = sem("acc_read")
        sumsq_done = sem("sumsq_done")
        meansq_done = sem("meansq_done")
        rstd_done = sem("rstd_done")
        normed = sem("normed")
        vec_step = sem("vec_step")
        act_step = sem("act_step")
        x_loaded = sem("x_loaded")
        small_loaded = sem("small_loaded")
        gain_loaded = [sem(f"gain_loaded{i}") for i in range(2)]
        pool_loaded = sem("pool_loaded")
        attn_loaded = sem("attn_loaded")
        rel_loaded = sem("rel_loaded")
        rel_turned = sem("rel_turned")
        rel_masked = sem("rel_masked")
        rel_stored = sem("rel_stored")
        rel_spread = sem("rel_spread")
        constants = sem("constants")
        product_hi = sem("product_hi")
        product_split = sem("product_split")
        squared = sem("squared")
        qk_mean = sem("qk_mean")
        qk_rstd = sem("qk_rstd")
        q_ready = sem("q_ready")
        max_done = sem("max_done")
        exp_done = sem("exp_done")
        stored = sem("stored")

        def bank(b, chunks):
            return turn[b][:, 0:chunks * P].rearrange("p (c k) -> p c k", c=chunks)

        block = ctx.enter_context(nc.Block())
        rows = lambda ap, n=P: ap.partition_broadcast(n)

        @block.sync
        def _(sp):
            def load_unit(n, s, wait):
                if wait is not None:
                    sp.wait_ge(lo_made, wait)
                sp.dma_start(raw[:, s, :], stream[n]).then_inc(raw_landed[s], 16)

            for t in range(HALVES):
                sp.dma_start(x[:, t, :], x_in[t * P:(t + 1) * P, :]).then_inc(x_loaded, 16)
            for s in range(RING):
                load_unit(s, s, None)
            with sp.Fori(1, units_total // RING) as i:
                for s in range(RING):
                    load_unit(i * RING + s, s, i * RING + (s + 1 - RING))
            sp.wait_ge(stored, 16 * HALVES)

        @block.gpsimd
        def _(pool):
            pool.dma_start(ident[:, :], ident_in).then_inc(small_loaded, 16)
            pool.dma_start(tap[:, :, :, :], taps).then_inc(small_loaded, 16)
            pool.memset(neg_half[:, :], -0.5).then_inc(constants, 1)
            for i in range(2):
                pool.dma_start(gain[:, i, :], rows(gains[i])).then_inc(gain_loaded[i], 16)
            pool.dma_start(onehot[:, :], onehot_in).then_inc(rel_loaded, 16)
            pool.dma_start(rel_in[:, :], rel_bias).then_inc(rel_loaded, 16)
            pool.dma_start(mask_rows[:, :], mask_in).then_inc(rel_loaded, 16)
            pool.dma_start(qk_gain[:, 0, :], rows(q_gain)).then_inc(attn_loaded, 16)
            pool.dma_start(qk_gain[:, 1, :], rows(k_gain)).then_inc(attn_loaded, 16)
            pool.dma_start(small[:, 0, 0:HEADS], rows(sinks)).then_inc(attn_loaded, 16)
            pool.dma_start(b_o_row[:, :], rows(b_o)).then_inc(attn_loaded, 16)
            pool.wait_ge(rel_masked, 1)
            pool.dma_start(table, rel_rows[:, :]).then_inc(rel_stored, 16)
            pool.wait_ge(rel_stored, 16)
            pool.dma_start(spread.rearrange("q (h k) -> h q k", h=HEADS),
                           bass.AP(table.tensor, P - 1, [[BAND, HEADS], [-1, P], [1, SEQ]])
                           ).then_inc(rel_stored, 16)
            pool.wait_ge(constants, 1)
            qk_done = 0
            for ph in phases:
                for t in range(HALVES):
                    pool.wait_ge(meansq_done, 2 * ph.index + t + 1)
                    pool.tensor_tensor(rstd[:, t:t + 1], meansq[:, t:t + 1], neg_half[:, 0:1],
                                       ALU.pow).then_inc(rstd_done, 1)
                if ph.index and ph.index + 1 < len(phases):
                    i = (ph.index + 1) % 2
                    pool.wait_ge(normed, 2 * ph.index)
                    pool.dma_start(gain[:, i, :], rows(gains[ph.index + 1])).then_inc(gain_loaded[i], 16)
                if ph.kind == CONV and ph.layer == 0:
                    pool.wait_ge(product_split, 2 * (CONV_TILES - CV_TILES))
                    pool.dma_start(averaging, band_in).then_inc(pool_loaded, 16)
                    pool.dma_start(pool_rows[:, 0, :], rows(pool_b)).then_inc(pool_loaded, 16)
                    pool.dma_start(pool_rows[:, 1, :], rows(pool_scale)).then_inc(pool_loaded, 16)
                if ph.index and phases[ph.index - 1].kind == POOL:
                    pool.wait_ge(rel_stored, 32)
                    pool.wait_ge(acc_read, ph.acc)
                    pool.dma_start(rel.rearrange("p h k -> p (h k)"), spread).then_inc(rel_spread, 16)
                    pool.dma_start(bias_qkv[:, 0, :], rows(b_qkv)).then_inc(attn_loaded, 16)
                if ph.kind == ATTN:
                    for t in range(HALVES):
                        qk_done += 1
                        pool.wait_ge(qk_mean, qk_done)
                        pool.tensor_tensor(small[:, 2, :], small[:, 1, :], neg_half[:, :],
                                           ALU.pow).then_inc(qk_rstd, 1)

        @block.tensor
        def _(pe):
            def first(ins, release):
                if release:
                    ins.then_inc(unit_used, 1)

            def in_half(ph, i, t, unit, hi, lo, slots, cols=512, units=IN_UNITS, release=False):
                h = ph.into + i * 2 + t
                per = KC // units
                if not (isinstance(h, int) and h < 2):
                    pe.wait_ge(in_read, h - 1)
                for u in range(units):
                    s = slots[u]
                    for k in range(per):
                        c = u * per + k
                        if t == 0 and k == 0:
                            pe.wait_ge(hi_made, unit + (u + 1))
                        wh = w_hi[:, s, k * cols:(k + 1) * cols]
                        wl = w_lo[:, s, k * cols:(k + 1) * cols]
                        o = into[t][:, 0:cols]
                        m = pe.matmul(o, hi[:, t, c, :], wh, start=(c == 0), stop=False)
                        first(m, release and c == 0)
                        pe.matmul(o, lo[:, t, c, :], wh, start=False, stop=False)
                        if t == 0 and k == 0:
                            pe.wait_ge(lo_made, unit + (u + 1))
                        last = pe.matmul(o, hi[:, t, c, :], wl, start=False, stop=(c == KC - 1))
                    if t == 1 and u < units - 1:
                        last.then_inc(unit_used, 1)
                last.then_inc(in_done, 1)

            def turn_half(fill, source, chunks, ready, release=False):
                if ready is not None:
                    pe.wait_ge(*ready)
                f = fill[0] + fill[1]
                b = fill[2]
                if not (isinstance(f, int) and f < 2):
                    pe.wait_ge(turn_read, f - 1)
                for c in range(chunks):
                    last = pe.transpose(turn[b][:, c * P:(c + 1) * P], source[:, c * P:(c + 1) * P],
                                        ident[:, :])
                    if c == 0 and release:
                        assert chunks > 1
                        last.then_inc(unit_used, 1)
                last.then_inc(turned, 1)

            def out_unit(t, unit, s, hi, lo, k, start, stop, wait, release_prev=False):
                if wait:
                    pe.wait_ge(lo_made, unit + 1)
                for n, (stat, w) in enumerate(((hi, w_hi), (lo, w_hi), (hi, w_lo))):
                    for half in range(2):
                        cols = slice(half * 512, half * 512 + 512)
                        last = pe.matmul(accum[t][:, cols], stat[:, t, k, :], w[:, s, cols],
                                         start=(start and n == 0), stop=(stop and n == 2))
                        if n == 0 and half == 0 and release_prev:
                            last.then_inc(unit_used, 1)
                return last

            def norm_turns(ph, t, release):
                for q in range(2):
                    f = 2 * t + q
                    turn_half((ph.norm_fill, f, f % 2), xn[:, t, q * 512:(q + 1) * 512], 4,
                              (normed, 2 * ph.index + t + 1) if q == 0 else None,
                              release and q == 0)

            def out_blocks(ph, unit, first_block, ready, release):
                order = [(0, 0, 2), (1, 0, 2), (0, 2, KC), (1, 2, KC)]
                for t, k0, k1 in order:
                    if k0 == 0:
                        pe.wait_ge(*ready[t])
                        if ph.acc >= 2 or first_block:
                            pe.wait_ge(acc_read, ph.acc + first_block + t - 1)
                    for k in range(k0, k1):
                        n = unit + k
                        last = out_unit(t, n, n % RING, u_hi, u_lo, k, k == 0, k == KC - 1, t == 0,
                                        release_prev=(release and t == 0 and k == 0))
                        if t == 1 and k < KC - 1:
                            last.then_inc(unit_used, 1)
                        if k == KC - 1:
                            last.then_inc(acc_done, 1)

            def ffn(ph):
                def ring(at, n):
                    return [(ph.unit + at + u) % RING for u in range(n)]

                def in_both(j):
                    unit = ph.unit if isinstance(j, int) and j == 0 else \
                        ph.unit + IN_UNITS + (j - 1) * RING
                    slots = ring(0 if isinstance(j, int) and j == 0 else IN_UNITS, IN_UNITS)
                    for t in range(HALVES):
                        if isinstance(j, int) and j == 0:
                            if t == 1:
                                norm_turns(ph, 1, False)
                            pe.wait_ge(turn_read, ph.norm_fill + 2 * t + 2)
                        in_half(ph, j, t, unit, h_hi, h_lo, slots)

                def turns(j, release=False):
                    for t in range(HALVES):
                        turn_half((ph.fill + t, j * 2, t), act[:, t, :], 2,
                                  (in_read, ph.into + (j * 2 + (t + 1))), release and t == 0)

                def down(j, unit, at, first_j=False, last_j=False, release_prev=True):
                    slots = ring(at, OUT_UNITS)
                    for t in range(HALVES):
                        if first_j and ph.acc >= 2:
                            pe.wait_ge(acc_read, ph.acc + t - 1)
                        pe.wait_ge(turn_read, ph.fill + (j * 2 + (t + 1)))
                        for k in range(OUT_UNITS):
                            last = out_unit(t, unit + k, slots[k], u_hi, u_lo, k, first_j and k == 0,
                                            last_j and k == OUT_UNITS - 1, t == 0,
                                            release_prev and t == 0 and k == 0)
                            done = last_j and k == OUT_UNITS - 1
                            if done:
                                last.then_inc(acc_done, 1)
                            elif t == 1:
                                last.then_inc(unit_used, 1)

                in_both(0)
                turns(0, release=True)
                in_both(1)
                down(0, ph.unit + 2 * IN_UNITS, 2 * IN_UNITS, first_j=True)
                turns(1)
                with pe.Fori(2, FTILES) as j:
                    in_both(j)
                    down(j - 1, ph.unit + 2 * IN_UNITS + (j - 1) * RING, 2 * IN_UNITS)
                    turns(j)
                down(FTILES - 1, ph.unit + FFN_UNITS - OUT_UNITS, FFN_UNITS - OUT_UNITS, last_j=True,
                     release_prev=False)

            def conv_mixer(ph):
                def turns(i, t, release=False):
                    rows_of = act[:, t, :] if i < CV_TILES else b_rows[:, t, :]
                    turn_half((ph.fill, 2 * i + t, t), rows_of, 2 if i < CV_TILES else 4,
                              (in_read, ph.into + 2 * i + t + 1), release)

                for i in range(CONV_TILES):
                    unit = ph.unit + IN_UNITS * i
                    slots = [(unit + u) % RING for u in range(IN_UNITS)]
                    for t in range(HALVES):
                        if i == 0:
                            if t == 1:
                                norm_turns(ph, 1, False)
                            pe.wait_ge(turn_read, ph.norm_fill + 2 * t + 2)
                        in_half(ph, i, t, unit, h_hi, h_lo, slots)
                        if t == 1:
                            turns(i, 0, release=i < CONV_TILES - 1)
                        elif i:
                            turns(i - 1, 1)
                turns(CONV_TILES - 1, 1)
                n = 2 * (CONV_TILES - CV_TILES) * (1 + (ph.layer > 0))
                out_blocks(ph, ph.unit + CONV_TILES * IN_UNITS, 0,
                           [(product_split, n - 1), (product_split, n)], release=True)

            def pool_mixer(ph):
                pe.wait_ge(pool_loaded, 48)
                for q in range(4):
                    f = ph.norm_fill + q
                    if q == 0:
                        pe.wait_ge(normed, 2 * ph.index + 2)
                    pe.wait_ge(turn_read, f - 1)
                    for k in range(2):
                        c = 2 * q + k
                        bank = turn[q % 2]
                        m = pe.matmul(bank[:, k * SEQ:(k + 1) * SEQ], xn[:, 0, c * P:(c + 1) * P],
                                      averaging[:, q, 0, :], start=True, stop=False)
                        if c == 0:
                            first(m, True)
                        last = pe.matmul(bank[:, k * SEQ + P:(k + 1) * SEQ], xn[:, 1, c * P:(c + 1) * P],
                                         averaging[:, q, 1, P:SEQ], start=False, stop=True)
                    last.then_inc(turned, 1)
                for t in range(HALVES):
                    pe.wait_ge(acc_read, ph.acc + t - 1)
                    for g in range(4):
                        if t == 0:
                            pe.wait_ge(turn_read, ph.norm_fill + g + 1)
                            pe.wait_ge(lo_made, ph.unit + g // 2 + 1)
                        s = (ph.unit + g // 2) % RING
                        o = accum[t][:, g * FT:(g + 1) * FT]
                        for k in range(2):
                            c = 2 * g + k
                            cols = slice(((g % 2) * 2 + k) * FT, ((g % 2) * 2 + k + 1) * FT)
                            pe.matmul(o, h_hi[:, t, c, :], w_hi[:, s, cols], start=(k == 0), stop=False)
                            pe.matmul(o, h_lo[:, t, c, :], w_hi[:, s, cols], start=False, stop=False)
                            last = pe.matmul(o, h_hi[:, t, c, :], w_lo[:, s, cols], start=False,
                                             stop=(k == 1))
                        if t == 1 and g == 1:
                            last.then_inc(unit_used, 1)
                    last.then_inc(acc_done, 1)

            def attn_mixer(ph):
                unit = ph.unit
                for i in range(3):
                    units = IN_UNITS if i < 2 else KV_UNITS
                    slots = [(unit + u) % RING for u in range(units)]
                    for t in range(HALVES):
                        if i == 0:
                            if t == 1:
                                norm_turns(ph, 1, False)
                            pe.wait_ge(turn_read, ph.norm_fill + 2 * t + 2)
                        in_half(ph, i, t, unit, h_hi, h_lo, slots, 512 if i < 2 else 256, units,
                                release=(i > 0 and t == 0))
                    unit += units
                f = 0
                for t in range(HALVES):
                    for q in range(2):
                        turn_half((ph.fill, f, f % 2), xn[:, t, q * 512:(q + 1) * 512], 4,
                                  (q_ready, KV_HEADS * (t + 1)) if q == 0 else None,
                                  release=(f == 0))
                        f += 1
                    turn_half((ph.fill, f, f % 2), k_twice.rearrange("p a b -> p (a b)"), 2, None)
                    f += 1
                h = ph.into + 6
                pe.wait_ge(turn_read, ph.fill + 6)
                for t in range(HALVES):
                    keys = (t + 1) * P
                    for b in range(HEADS // 2):
                        pe.wait_ge(in_read, h - 1)
                        odd = b % 2
                        for m in range(2):
                            head = 4 * (b // 2) + 2 * m + odd
                            last = pe.matmul(into[h % 2][:, m * SEQ:m * SEQ + keys],
                                             q_t[odd * HD:(odd + 1) * HD, t, head // 2, :],
                                             k_t[odd * HD:(odd + 1) * HD, head // 8, 0:keys],
                                             start=True, stop=True)
                        last.then_inc(in_done, 1)
                        h += 1
                    blocks = [(head, kb) for head in range(HEADS) for kb in range(t + 1)]
                    for g in range(len(blocks) // 4):
                        heads = [blocks[4 * g + m][0] for m in range(4)]
                        pe.wait_ge(exp_done, t * HEADS + heads[-1] + 1)
                        pe.wait_ge(turn_read, ph.fill + f - 1)
                        for m in range(4):
                            head, kb = blocks[4 * g + m]
                            last = pe.transpose(turn[f % 2][:, m * P:(m + 1) * P],
                                                scores[:, head, kb * P:(kb + 1) * P], ident[:, :])
                        last.then_inc(turned, 1)
                        f += 1
                    pe.wait_ge(turn_read, ph.fill + f)
                    pe.wait_ge(acc_read, ph.acc + t - 1)
                    for n, (head, kb) in enumerate(blocks):
                        v = qkv[:, kb, NQK * HD + (head // 8) * HD:NQK * HD + (head // 8 + 1) * HD]
                        last = pe.matmul(accum[t][:, head * HD:(head + 1) * HD], probs_t[:, n, :], v,
                                         start=(kb == 0), stop=(kb == t))
                    last.then_inc(acc_done, 1)
                for t in range(HALVES):
                    for q in range(2):
                        turn_half((ph.fill, f, f % 2), xn[:, t, q * 512:(q + 1) * 512], 4,
                                  (acc_read, ph.acc + t + 1))
                        f += 1
                assert f == FILLS[ATTN]
                out_blocks(ph, unit, 2, [(turn_read, ph.fill + f - 2), (turn_read, ph.fill + f)], release=False)

            pe.wait_ge(rel_loaded, 48)
            pe.matmul(accum[0][0:HEADS, 0:BAND], rel_in[:, :], onehot[:, :], start=True,
                      stop=True).then_inc(rel_turned, 1)
            pe.wait_ge(small_loaded, 32)
            pe.wait_ge(rel_masked, 1)
            for ph in phases:
                if ph.kind != POOL:
                    norm_turns(ph, 0, release=ph.index > 0)
                if ph.kind == FFN:
                    ffn(ph)
                elif ph.kind == CONV:
                    conv_mixer(ph)
                elif ph.kind == POOL:
                    pool_mixer(ph)
                else:
                    attn_mixer(ph)

        @block.scalar
        def _(sc):
            def hi_unit(n, s, landed, wait):
                sc.wait_ge(raw_landed[s], landed)
                if wait is not None:
                    sc.wait_ge(unit_used, wait)
                sc.activation(w_hi[:, s, :], raw[:, s, :], ACT.Copy).then_inc(hi_made, 1)

            def hi_units(n0, n1):
                for n in range(n0, n1):
                    hi_unit(n, n % RING, 16 * (n // RING + 1), n - RING + 1 if n >= RING else None)

            def turn_split(b, to, f):
                sc.wait_ge(turned, f)
                sc.activation(to, bank(b, to.shape[1]), ACT.Copy).then_inc(turn_hi, 1)

            def boundary(ph, split_from):
                split_to = min(ph.unit + IN_UNITS, units_total)
                for t in range(HALVES):
                    if ph.index:
                        sc.wait_ge(acc_read, ph.acc - 1 + t)
                    else:
                        sc.wait_ge(x_loaded, 32)
                    sc.activation(xn[:, t, :], x[:, t, :], ACT.Square,
                                  accum_out=sumsq[:, t:t + 1]).then_inc(sumsq_done, 1)
                    if t == 0:
                        hi_units(split_from, split_to)
                    if ph.kind != POOL:
                        for q in range(2):
                            f = 2 * t + q
                            turn_split(f % 2, h_hi[:, t, 4 * q:4 * q + 4, :], ph.norm_fill + f + 1)

            def ffn(ph):
                def tile(j, hi):
                    for t in range(HALVES):
                        sc.wait_ge(in_done, ph.into + (j * 2 + (t + 1)))
                        sc.activation(gated[:, t, :], into[t][:, 0:FT], ACT.Silu).then_inc(gate_done, 1)
                        if hi and t == 0:
                            ahead(j, 0, IN_UNITS)
                    ahead(j, IN_UNITS, RING) if hi else \
                        hi_units(ph.next_unit - OUT_UNITS, ph.next_unit)
                    for t in range(HALVES):
                        turn_split(t, u_hi[:, t, 0:2, :], ph.fill + (j * 2 + (t + 1)))

                def ahead(j, a, b):
                    for u in range(a, b):
                        at = ph.unit + IN_UNITS + u
                        if isinstance(j, int):
                            hi_units(at + RING * j, at + RING * j + 1)
                        else:
                            hi_unit(None, at % RING, (j + (at // RING + 1)) * 16, j * RING + (at - RING + 1))

                tile(0, True)
                with sc.Fori(1, FTILES - 1) as j:
                    tile(j, True)
                tile(FTILES - 1, False)

            def conv_mixer(ph):
                out0 = ph.unit + CONV_TILES * IN_UNITS
                nth = 2 * (CONV_TILES - CV_TILES) * (ph.layer > 0)

                def product_split_hi(k, t):
                    sc.wait_ge(turn_read, ph.fill + 2 * (CV_TILES + k) + t + 1)
                    sc.activation(u_hi[:, t, 4 * k:4 * k + 4, :], gated_t[:, t, :],
                                  ACT.Copy).then_inc(product_hi, 1)

                for i in range(CONV_TILES):
                    nxt = ph.unit + IN_UNITS * (i + 1)
                    for t in range(HALVES):
                        if i < CV_TILES:
                            sc.wait_ge(in_done, ph.into + 2 * i + t + 1)
                            sc.activation(gated[:, t, :], into[t][:, 0:FT], ACT.Copy).then_inc(gate_done, 1)
                        if t == 0:
                            hi_units(nxt, nxt + IN_UNITS)
                    if i >= CV_TILES:
                        product_split_hi(i - CV_TILES, 0)
                        if i == CONV_TILES - 1:
                            hi_units(out0 + 4, out0 + 6)
                        product_split_hi(i - CV_TILES, 1)
                hi_units(out0 + 6, out0 + KC)

            def pool_mixer(ph):
                for q in range(4):
                    sc.wait_ge(turned, ph.norm_fill + q + 1)
                    sc.activation(h_hi[:, :, 2 * q:2 * q + 2, :].rearrange("p t c k -> p c t k"),
                                  turn[q % 2][:, :].rearrange("p (c t k) -> p c t k", c=2, t=2),
                                  ACT.Copy).then_inc(turn_hi, 1)

            def attn_mixer(ph):
                q1 = ph.unit + IN_UNITS
                kv = q1 + IN_UNITS
                out0 = kv + KV_UNITS
                hi_units(q1, out0 + 4)
                for t in range(HALVES):
                    sc.wait_ge(in_read, ph.into + 4 + t + 1)
                    if t:
                        sc.wait_ge(qk_mean, t)
                    sc.activation(qk_sq[:, 0, :], qkv[:, t, 0:NQK * HD], ACT.Square).then_inc(squared, 1)
                hi_units(out0 + 4, out0 + 6)
                for t in range(HALVES):
                    sc.wait_ge(max_done, t + 1)
                    sc.activation(small[:, 5, 0:HEADS], small[:, 4, 0:HEADS], ACT.Exp).then_inc(act_step, 1)
                    for head in range(HEADS):
                        keys = scores[:, head, 0:(t + 1) * P]
                        sc.activation(keys, keys, ACT.Exp, bias=small[:, 3, head:head + 1],
                                      accum_out=small[:, 6, head:head + 1]).then_inc(exp_done, 1)
                f = ph.fill + FILLS[ATTN] - 4
                for t in range(HALVES):
                    for q in range(2):
                        f += 1
                        turn_split((f - 1) % 2, u_hi[:, t, 4 * q:4 * q + 4, :], f)
                hi_units(out0 + 6, out0 + KC)

            nxt = 0
            for ph in phases:
                boundary(ph, nxt)
                nxt = ph.unit + IN_UNITS
                if ph.kind == FFN:
                    ffn(ph)
                elif ph.kind == CONV:
                    conv_mixer(ph)
                elif ph.kind == POOL:
                    pool_mixer(ph)
                else:
                    attn_mixer(ph)
                if ph.kind != POOL:
                    nxt = ph.next_unit
            for t in range(HALVES):
                sc.wait_ge(acc_read, phases[-1].acc + t + 1)
                sc.dma_start(out[t * P:(t + 1) * P, :], x[:, t, :]).then_inc(stored, 16)

        @block.vector
        def _(ve):
            steps = [0]

            def link(ins, sem=None, count=None):
                if sem is None:
                    steps[0] += 1
                    sem, count = vec_step, steps[0]
                ins.then_inc(sem, 1)
                ve.wait_ge(sem, count)

            def lo_unit(s, made):
                ve.wait_ge(hi_made, made)
                ve.tensor_tensor(w_lo[:, s, :], raw[:, s, :], w_hi[:, s, :].bitcast(F32),
                                 ALU.subtract).then_inc(lo_made, 1)

            def lo_units(n0, n1):
                for n in range(n0, n1):
                    lo_unit(n % RING, n + 1)

            turn_his = [0]

            def turn_split(b, to, hi, count):
                ve.wait_ge(turn_hi, count)
                ve.tensor_tensor(to, bank(b, to.shape[1]), hi.bitcast(F32),
                                 ALU.subtract).then_inc(turn_read, 1)

            def residual(ph, t, acc):
                ve.wait_ge(acc_done, acc + 1)
                if ph.kind == POOL:
                    link(ve.tensor_tensor(pool_y[:, t, :], accum[t][:, :], pool_rows[:, 0, :], ALU.add))
                    link(ve.tensor_tensor(pool_y[:, t, :], pool_y[:, t, :], pool_rows[:, 1, :], ALU.mult))
                    ve.tensor_tensor(x[:, t, :], pool_y[:, t, :], x[:, t, :], ALU.add).then_inc(acc_read, 1)
                else:
                    ve.scalar_tensor_tensor(out=x[:, t, :], in0=accum[t][:, :],
                                            scalar=0.5 if ph.kind == FFN else 1.0, in1=x[:, t, :],
                                            op0=ALU.mult, op1=ALU.add).then_inc(acc_read, 1)

            def boundary(prev, ph, split_from):
                split_to = min(ph.unit + IN_UNITS, units_total)

                def mean(t):
                    ve.wait_ge(sumsq_done, 2 * ph.index + t + 1)
                    ve.tensor_scalar(meansq[:, t:t + 1], sumsq[:, t:t + 1], 1.0 / D, EPS, ALU.mult,
                                     ALU.add).then_inc(meansq_done, 1)

                def normalize(t):
                    ve.wait_ge(rstd_done, 2 * ph.index + t + 1)
                    g = ph.index % 2
                    ve.wait_ge(gain_loaded[g], 16 * (ph.index // 2 + 1))
                    ve.scalar_tensor_tensor(out=xn[:, t, :], in0=x[:, t, :], scalar=rstd[:, t:t + 1],
                                            in1=gain[:, g, :], op0=ALU.mult,
                                            op1=ALU.mult).then_inc(normed, 1)

                def splits(t):
                    if ph.kind != POOL:
                        for q in range(2):
                            turn_his[0] += 1
                            turn_split(q, h_lo[:, t, 4 * q:4 * q + 4, :], h_hi[:, t, 4 * q:4 * q + 4, :],
                                       turn_his[0])

                if prev is not None:
                    residual(prev, 0, ph.acc - 2)
                mean(0)
                n = split_from
                lo_units(n, min(n + 1, split_to))
                normalize(0)
                lo_units(min(n + 1, split_to), split_to)
                if prev is not None:
                    residual(prev, 1, ph.acc - 1)
                splits(0)
                mean(1)
                normalize(1)
                splits(1)

            def ffn(ph):
                his = turn_his[0]

                def tile(j, lo):
                    for t in range(HALVES):
                        ve.wait_ge(gate_done, gates[0] + (j * 2 + (t + 1)))
                        ve.tensor_tensor(act[:, t, :], gated[:, t, :], into[t][:, FT:2 * FT],
                                         ALU.mult).then_inc(in_read, 1)
                        if lo and t == 0:
                            ahead(j, 0, IN_UNITS)
                    ahead(j, IN_UNITS, RING) if lo else \
                        lo_units(ph.next_unit - OUT_UNITS, ph.next_unit)
                    for t in range(HALVES):
                        turn_split(t, u_lo[:, t, 0:2, :], u_hi[:, t, 0:2, :], his + (j * 2 + (t + 1)))

                def ahead(j, a, b):
                    for u in range(a, b):
                        at = ph.unit + IN_UNITS + u
                        lo_unit(at % RING, j * RING + (at + 1))

                tile(0, True)
                with ve.Fori(1, FTILES - 1) as j:
                    tile(j, True)
                tile(FTILES - 1, False)
                gates[0] += 2 * FTILES
                turn_his[0] += 2 * FTILES

            def conv_mixer(ph):
                w = tap[:, int(ph.layer > 0), :, :]
                nth = 2 * (CONV_TILES - CV_TILES) * (ph.layer > 0)
                out0 = ph.unit + CONV_TILES * IN_UNITS
                done = CONV_TILES * 2

                link(ve.memset(z_t[:, :, 0:TAPS - 1], 0.0))

                def z_turned(i, t):
                    ve.wait_ge(turned, ph.fill + 2 * i + t + 1)
                    a = TAPS - 1 + t * P
                    link(ve.tensor_copy(z_t[:, 2 * i:2 * i + 2, a:a + P], bank(t, 2)),
                         turn_read, ph.fill + 2 * i + t + 1)

                def convolve(i):
                    for tp in range(TAPS):
                        for c in (2 * i, 2 * i + 1):
                            z = z_t[:, c, tp:tp + SEQ]
                            o = conv[:, c, :]
                            if tp == 0:
                                ins = ve.tensor_scalar(o, z, w[:, tp, c:c + 1], None, ALU.mult)
                            else:
                                ins = ve.scalar_tensor_tensor(out=o, in0=z, scalar=w[:, tp, c:c + 1],
                                                              in1=o, op0=ALU.mult, op1=ALU.add)
                            if c % 2:
                                link(ins)
                            else:
                                steps[0] += 1
                                ins.then_inc(vec_step, 1)

                def product(k, t):
                    f = ph.fill + 2 * (CV_TILES + k) + t + 1
                    ve.wait_ge(turned, f)
                    if k:
                        ve.wait_ge(product_hi, nth + 2 * (k - 1) + t + 1)
                    link(ve.tensor_tensor(gated_t[:, t, :].rearrange("p (c k) -> p c k", c=4), bank(t, 4),
                                          conv[:, 4 * k:4 * k + 4, t * P:(t + 1) * P], ALU.mult),
                         turn_read, f)

                def product_lo(k, t):
                    ve.wait_ge(product_hi, nth + 2 * k + t + 1)
                    ve.tensor_tensor(u_lo[:, t, 4 * k:4 * k + 4, :],
                                     gated_t[:, t, :].rearrange("p (c k) -> p c k", c=4),
                                     u_hi[:, t, 4 * k:4 * k + 4, :].bitcast(F32),
                                     ALU.subtract).then_inc(product_split, 1)

                for i in range(CONV_TILES):
                    nxt = ph.unit + IN_UNITS * (i + 1)
                    for t in range(HALVES):
                        if i < CV_TILES:
                            ve.wait_ge(gate_done, gates[0] + 2 * i + t + 1)
                            ve.tensor_tensor(act[:, t, :], gated[:, t, :], into[t][:, FT:2 * FT],
                                             ALU.mult).then_inc(in_read, 1)
                        else:
                            ve.wait_ge(in_done, ph.into + 2 * i + t + 1)
                            ve.tensor_copy(b_rows[:, t, :], into[t][:, :]).then_inc(in_read, 1)
                        if t == 0:
                            if 0 < i:
                                if i <= CV_TILES:
                                    z_turned(i - 1, 1)
                                    convolve(i - 1)
                                else:
                                    product(i - 1 - CV_TILES, 1)
                                    product_lo(i - 1 - CV_TILES, 1)
                            if i < CONV_TILES - 1:
                                lo_units(nxt, nxt + IN_UNITS)
                            else:
                                lo_units(nxt, nxt + IN_UNITS)
                    if i < CV_TILES:
                        z_turned(i, 0)
                    else:
                        product(i - CV_TILES, 0)
                        product_lo(i - CV_TILES, 0)
                product(1, 1)
                lo_units(out0 + 4, out0 + 6)
                product_lo(1, 1)
                lo_units(out0 + 6, out0 + KC)
                gates[0] += 2 * CV_TILES

            def pool_mixer(ph):
                for q in range(4):
                    turn_his[0] += 1
                    pool_split(q, turn_his[0])

            def pool_split(q, count):
                ve.wait_ge(turn_hi, count)
                o = h_lo[:, :, 2 * q:2 * q + 2, :].rearrange("p t c k -> p c t k")
                i = h_hi[:, :, 2 * q:2 * q + 2, :].rearrange("p t c k -> p c t k").bitcast(F32)
                ve.tensor_tensor(o, turn[q % 2][:, :].rearrange("p (c t k) -> p c t k", c=2, t=2), i,
                                 ALU.subtract).then_inc(turn_read, 1)

            def attn_mixer(ph):
                q1 = ph.unit + IN_UNITS
                out0 = q1 + IN_UNITS + KV_UNITS
                ve.wait_ge(attn_loaded, 16 * 5)
                for i in range(3):
                    n = 512 if i < 2 else 256
                    for t in range(HALVES):
                        ve.wait_ge(in_done, ph.into + 2 * i + t + 1)
                        ve.tensor_tensor(qkv[:, t, 512 * i:512 * i + n], into[t][:, 0:n],
                                         bias_qkv[:, 0, 512 * i:512 * i + n], ALU.add).then_inc(in_read, 1)
                        if t == 0:
                            if i == 0:
                                lo_units(q1, q1 + 4)
                            elif i == 1:
                                lo_units(q1 + 4, q1 + 6)
                for t in range(HALVES):
                    link(ve.tensor_tensor(x[:, t, :], x[:, t, :], b_o_row[:, :], ALU.add))
                lo_units(out0, out0 + 4)
                for t in range(HALVES):
                    ve.wait_ge(squared, t + 1)
                    link(ve.tensor_reduce(small[:, 1, :], qk_sq[:, 0, :].rearrange("p (h d) -> p h d", d=HD),
                                          AX.X, ALU.add))
                    ve.tensor_scalar(small[:, 1, :], small[:, 1, :], 1.0 / HD, EPS, ALU.mult,
                                     ALU.add).then_inc(qk_mean, 1)
                    ve.wait_ge(qk_rstd, t + 1)
                    heads = qkv[:, t, 0:NQK * HD].rearrange("p (h d) -> p h d", d=HD)
                    link(ve.tensor_tensor(heads, heads,
                                          small[:, 2, :].unsqueeze(2).broadcast_to([P, NQK, HD]), ALU.mult))
                    if t:
                        ve.wait_ge(turned, ph.fill + 3)
                    ve.tensor_tensor(xn[:, t, :].rearrange("p (h d) -> p h d", d=HD), heads[:, 0:HEADS, :],
                                     qk_gain[:, 0, :].unsqueeze(1).broadcast_to([P, HEADS, HD]),
                                     ALU.mult).then_inc(vec_step, 1)
                    steps[0] += 1
                    for kv in range(KV_HEADS):
                        ve.tensor_tensor(k_twice[:, kv, :].rearrange("p (a d) -> p a d", a=2),
                                         heads[:, HEADS + kv:HEADS + kv + 1, :].broadcast_to([P, 2, HD]),
                                         qk_gain[:, 1, :].unsqueeze(1).broadcast_to([P, 2, HD]),
                                         ALU.mult).then_inc(q_ready, 1)
                    for q in range(2):
                        f = 3 * t + q
                        ve.wait_ge(turned, ph.fill + f + 1)
                        ve.tensor_copy(q_t[:, t, 4 * q:4 * q + 4, :],
                                       turn[f % 2][:, :].rearrange("p (c k) -> p c k", c=4)
                                       ).then_inc(turn_read, 1)
                    f = 3 * t + 2
                    ve.wait_ge(turned, ph.fill + f + 1)
                    ve.tensor_copy(k_t[:, :, t * P:(t + 1) * P],
                                   turn[f % 2][:, 0:2 * P].rearrange("p (c k) -> p c k", c=2)
                                   ).then_inc(turn_read, 1)
                lo_units(out0 + 4, out0 + 6)
                ve.wait_ge(rel_spread, 16)
                h = ph.into + 6
                f = ph.fill + 6
                for t in range(HALVES):
                    keys = (t + 1) * P
                    if t:
                        ve.wait_ge(turned, f)
                    for b in range(HEADS // 2):
                        h += 1
                        ve.wait_ge(in_done, h)
                        h0 = 4 * (b // 2) + b % 2
                        ve.scalar_tensor_tensor(
                            out=scores[:, h0:h0 + 3:2, 0:keys],
                            in0=into[(h - 1) % 2][:, :].rearrange("p (a k) -> p a k", a=2)[:, :, 0:keys],
                            scalar=HD ** -0.5, in1=rel[:, h0:h0 + 3:2, SEQ - keys:SEQ],
                            op0=ALU.mult, op1=ALU.add).then_inc(in_read, 1)
                    ve.wait_ge(in_read, h)
                    link(ve.tensor_reduce(small[:, 7, 0:HEADS], scores[:, :, 0:keys], AX.X, ALU.max))
                    link(ve.tensor_tensor(small[:, 7, 0:HEADS], small[:, 7, 0:HEADS], small[:, 0, 0:HEADS],
                                          ALU.max))
                    link(ve.tensor_scalar(small[:, 3, 0:HEADS], small[:, 7, 0:HEADS], -1.0, None, ALU.mult))
                    ve.tensor_tensor(small[:, 4, 0:HEADS], small[:, 0, 0:HEADS], small[:, 3, 0:HEADS],
                                     ALU.add).then_inc(max_done, 1)
                    for g in range(4 * (t + 1)):
                        f += 1
                        ve.wait_ge(turned, f)
                        if t and g == 0:
                            ve.wait_ge(acc_done, ph.acc + 1)
                        ve.tensor_copy(probs_t[:, 4 * g:4 * g + 4, :],
                                       turn[(f - 1) % 2][:, :].rearrange("p (c k) -> p c k", c=4)
                                       ).then_inc(turn_read, 1)
                    ve.wait_ge(act_step, t + 1)
                    ve.wait_ge(exp_done, HEADS * (t + 1))
                    link(ve.tensor_tensor(small[:, 8, 0:HEADS], small[:, 6, 0:HEADS], small[:, 5, 0:HEADS],
                                          ALU.add))
                    link(ve.reciprocal(small[:, 9, 0:HEADS], small[:, 8, 0:HEADS]))
                    ve.wait_ge(acc_done, ph.acc + t + 1)
                    ve.tensor_tensor(xn[:, t, :].rearrange("p (h d) -> p h d", d=HD),
                                     accum[t][:, :].rearrange("p (h d) -> p h d", d=HD),
                                     small[:, 9, 0:HEADS].unsqueeze(2).broadcast_to([P, HEADS, HD]),
                                     ALU.mult).then_inc(acc_read, 1)
                for t in range(HALVES):
                    for q in range(2):
                        f += 1
                        turn_his[0] += 1
                        turn_split((f - 1) % 2, u_lo[:, t, 4 * q:4 * q + 4, :],
                                   u_hi[:, t, 4 * q:4 * q + 4, :], turn_his[0])
                lo_units(out0 + 6, out0 + KC)

            ve.wait_ge(rel_turned, 1)
            ve.tensor_tensor(rel_rows[:, :], accum[0][0:HEADS, 0:BAND], mask_rows[:, :],
                             ALU.add).then_inc(rel_masked, 1)
            ve.wait_ge(small_loaded, 32)
            ve.wait_ge(x_loaded, 32)
            gates = [0]
            nxt = 0
            prev = None
            for ph in phases:
                boundary(prev, ph, nxt)
                nxt = ph.unit + IN_UNITS
                if ph.kind == FFN:
                    ffn(ph)
                elif ph.kind == CONV:
                    conv_mixer(ph)
                elif ph.kind == POOL:
                    pool_mixer(ph)
                else:
                    attn_mixer(ph)
                if ph.kind != POOL:
                    nxt = ph.next_unit
                prev = ph
            for t in range(HALVES):
                residual(prev, t, prev.acc + t)


def _buckets():
    import math

    import numpy as np

    dist = 255 - np.arange(BAND)
    inside = (dist >= 0) & (dist < 128)
    n = np.where(inside, dist, 0)
    nf = np.maximum(n, 1).astype(np.float32)
    large = 16 + (np.log(nf / 16) / math.log(128 / 16) * 16).astype(np.int32)
    bucket = np.where(n < 16, n, np.minimum(large, 31)).astype(np.int32)
    onehot = np.zeros((32, BAND), np.float32)
    onehot[bucket[inside], np.nonzero(inside)[0]] = 1.0
    mask = np.where(inside, 0.0, -1e30).astype(np.float32)
    return onehot, np.ascontiguousarray(np.broadcast_to(mask, (HEADS, BAND)))


def _averaging():
    import numpy as np

    m = np.zeros((P, 4, 2, SEQ), np.float32)
    for g, win in enumerate(POOL_WINDOWS):
        for s in range(SEQ):
            for r in range(max(0, s - win + 1), s + 1):
                m[r % P, g, r // P, s] += np.float32(1.0 / min(s + 1, win))
            m[s % P, g, s // P, s] -= 1.0
    return m


def _stream(a):
    import numpy as np

    def wide(w, groups, tiles, width):
        w = w.reshape(-1, UNIT // (groups * width), P, groups, tiles, width)
        return w.transpose(4, 0, 2, 1, 3, 5).reshape(-1, P, UNIT)

    def ffn(w_in, w_out):
        a_in = wide(w_in, 2, FTILES, FT).reshape(FTILES, IN_UNITS, P, UNIT)
        a_out = w_out.reshape(FTILES, OUT_UNITS, P, UNIT)
        parts = [a_in[0]]
        for j in range(1, FTILES):
            parts += [a_in[j], a_out[j - 1]]
        return parts + [a_out[FTILES - 1]]

    def conv(w_in, w_out):
        return [wide(w_in[:, D:], 2, CV_TILES, FT), wide(w_in[:, :D], 1, 2, 512),
                w_out.reshape(KC, P, UNIT)]

    def pool(w):
        return [w.reshape(2, 2, 2, P, FT).transpose(0, 3, 1, 2, 4).reshape(2, P, UNIT)]

    def attn(w_qkv, w_o):
        return [wide(w_qkv[:, :D], 1, 2, 512), wide(w_qkv[:, D:], 1, 1, 256), w_o.reshape(KC, P, UNIT)]

    parts = []
    for layer in range(DEPTH):
        parts += ffn(a["ffn1_w_in"][layer], a["ffn1_w_out"][layer])
        if layer % 3 == 0:
            parts += conv(a["conv_w_in"][layer // 3], a["conv_w_out"][layer // 3])
        elif layer % 3 == 1:
            parts += pool(a["pool_w"][0])
        else:
            parts += attn(a["attn_w_qkv"][0], a["attn_w_o"][0])
        parts += ffn(a["ffn2_w_in"][layer], a["ffn2_w_out"][layer])
    return np.concatenate(parts)


def kernel(**inputs):
    import concourse.bacc as bacc
    import numpy as np
    from concourse.bass_utils import run_bass_kernel_spmd

    a = {k: np.asarray(v) for k, v in inputs.items()}
    onehot, mask = _buckets()
    arrays = {
        "stream": _stream(a),
        "x_in": a["x"].reshape(SEQ, D),
        "gains": np.stack([a["ffn1_norm"], a["mix_norm"], a["ffn2_norm"]], 1).reshape(3 * DEPTH, D),
        "taps": a["conv_w"].reshape(2, TAPS, KC, P).transpose(3, 0, 1, 2),
        "pool_b": a["pool_b"][0],
        "pool_scale": a["pool_scale"][0],
        "b_qkv": a["attn_b_qkv"][0],
        "q_gain": a["attn_q_norm"][0],
        "k_gain": a["attn_k_norm"][0],
        "sinks": a["attn_sinks"][0],
        "b_o": a["attn_b_o"][0],
        "rel_bias": a["rel_bias"],
        "ident_in": np.eye(P, dtype=np.float32),
        "band_in": _averaging(),
        "onehot_in": onehot,
        "mask_in": mask,
    }
    arrays = {k: np.ascontiguousarray(v) for k, v in arrays.items()}
    nc = bacc.Bacc("TRN2", target_bir_lowering=False, num_devices=1)
    args = {k: nc.dram_tensor(k, v.shape, mybir.dt.from_np(v.dtype), kind="ExternalInput").ap()
            for k, v in arrays.items()}
    args["table"] = nc.dram_tensor("table", (HEADS, BAND), F32, kind="Internal").ap()
    args["spread"] = nc.dram_tensor("spread", (P, HEADS * SEQ), F32, kind="Internal").ap()
    args["out"] = nc.dram_tensor("y", (SEQ, D), F32, kind="ExternalOutput").ap()
    build(nc, **args)
    r = run_bass_kernel_spmd(nc, [arrays], core_ids=[0])
    return r.results[0]["y"].reshape(1, SEQ, D)
```

```python
from contextlib import ExitStack

import concourse.bass as bass
from concourse import mybir

F32 = mybir.dt.float32
F32R = mybir.dt.float32r
ALU = mybir.AluOpType
ACT = mybir.ActivationFunctionType
AX = mybir.AxisListType

P = 128
D = 1024
SEQ = 256
DEPTH = 4
DFF = 2816
HALVES = SEQ // P
KC = D // P
UNIT = 1024
RING = 6
FT = 256
FTILES = DFF // FT
IN_UNITS = KC * 2 * FT // UNIT
OUT_UNITS = 2
FFN_UNITS = FTILES * (IN_UNITS + OUT_UNITS)
B_TILES = 2
CV_TILES = 4
CONV_TILES = B_TILES + CV_TILES
CONV_UNITS = CONV_TILES * IN_UNITS + KC
POOL_UNITS = 2
POOL_WINDOWS = (2, 4, 8, 16)
HEADS = 16
KV_HEADS = 2
HD = 64
QKV = (HEADS + 2 * KV_HEADS) * HD
NQK = HEADS + KV_HEADS
KV_UNITS = 2
Q_HEADS = HEADS // 2
ITEMS = 6
ATTN_UNITS = 2 * IN_UNITS + KV_UNITS + KC
BAND = 384
EPS = 1e-6
TAPS = 3

FFN, CONV, POOL, ATTN = "ffn", "conv", "pool", "attn"
UNITS = {FFN: FFN_UNITS, CONV: CONV_UNITS, POOL: POOL_UNITS, ATTN: ATTN_UNITS}
INS = {FFN: 2 * FTILES, CONV: 2 * CONV_TILES, POOL: 0, ATTN: ITEMS + HEADS}
FILLS = {FFN: 2 * FTILES, CONV: 2 * CONV_TILES, POOL: 0, ATTN: 6 + 4 + 8 + 4}
ACCS = {FFN: 2, CONV: 2, POOL: 2, ATTN: 4}
NORM_FILLS = 4


class Phase:

    def __init__(self, kind, index, layer, before):
        self.kind, self.index, self.layer = kind, index, layer
        self.nth = layer // 3 if kind == CONV else 0
        self.unit = before.unit + UNITS[before.kind] if before else 0
        self.into = before.into + INS[before.kind] if before else 0
        self.norm_fill = before.fill + FILLS[before.kind] if before else 0
        self.fill = self.norm_fill + NORM_FILLS
        self.acc = before.acc + ACCS[before.kind] if before else 0
        self.next_unit = self.unit + UNITS[kind]


def make_phases():
    phases = []
    for layer, mixer in enumerate((CONV, POOL, ATTN, CONV)):
        for kind in (FFN, mixer, FFN):
            phases.append(Phase(kind, len(phases), layer, phases[-1] if phases else None))
    return phases


def build(nc, stream, x_in, gains, taps, pool_b, pool_scale, b_qkv, q_gain, k_gain, sinks, b_o,
          rel_bias, ident_in, band_in, onehot_in, mask_in, table, spread, out):
    phases = make_phases()
    units_total = phases[-1].next_unit
    assert units_total % RING == 0 and all(p.into % 2 == 0 and p.fill % 2 == 0 for p in phases)

    ctx = ExitStack()
    with ctx:
        def sb(name, shape, dt=F32):
            return ctx.enter_context(nc.sbuf_tensor(name, shape, dt))

        def sem(name):
            return ctx.enter_context(nc.semaphore(name))

        raw = sb("raw", [P, RING, UNIT])
        w_hi = sb("w_hi", [P, RING, UNIT], F32R)
        w_lo = sb("w_lo", [P, RING, UNIT], F32R)
        x = sb("x", [P, HALVES, D])
        xn = sb("xn", [P, HALVES, D])
        h_hi = sb("h_hi", [P, HALVES, KC, P], F32R)
        h_lo = sb("h_lo", [P, HALVES, KC, P], F32R)
        u_hi = sb("u_hi", [P, HALVES, KC, P], F32R)
        u_lo = sb("u_lo", [P, HALVES, KC, P], F32R)
        gain = sb("gain", [P, 2, D])
        squares = sb("squares", [P, HALVES, D], mybir.dt.bfloat16)
        meansq = sb("meansq", [P, HALVES])
        padded = sb("padded", [P, HALVES])
        rstd = sb("rstd", [P, HALVES])
        neg_half = sb("neg_half", [P, Q_HEADS])
        gated = sb("gated", [P, HALVES, FT])
        act = sb("act", [P, HALVES, FT])
        ident = sb("ident", [P, P])
        MIX = 15616
        mix = sb("mix", [P, MIX])
        tap = sb("tap", [P, 2, TAPS, KC])

        def part(at, *shape):
            n = 1
            for s in shape:
                n *= s
            assert at + n <= MIX
            names = " ".join("abc"[:len(shape)])
            kw = {c: s for c, s in zip("abc", shape)}
            return mix[:, at:at + n].rearrange(f"p ({names}) -> p {names}", **kw), at + n

        z_t, a = part(0, KC, SEQ + TAPS - 1)
        b_t, a = part(a, KC, SEQ)
        b_rows, a = part(a, HALVES, 512)
        product, a = part(a, 2, SEQ)
        averaging, a = part(0, 4, 2, SEQ)
        pool_rows, a = part(a, 2, D)
        pool_y, a = part(a, HALVES, D)
        rel_space, a = part(a, 3 * BAND + HEADS)
        onehot = rel_space[0:32, 0:BAND]
        rel_in = rel_space[0:32, 3 * BAND:3 * BAND + HEADS]
        mask_rows = rel_space[0:HEADS, BAND:2 * BAND]
        rel_rows = rel_space[0:HEADS, 2 * BAND:3 * BAND]
        rel, a = part(0, HEADS, SEQ)
        bias_qkv, b = part(a, 1, QKV)
        qk_sq, b = part(b, 2, 512)
        scores_1, a = part(a, HEADS, SEQ)
        probs_t, a = part(a, 32, P)
        qkv, a = part(a, HALVES, QKV)
        k_twice, a = part(a, KV_HEADS, P)
        k_t, a = part(a, KV_HEADS, SEQ)
        q_t = probs_t[:, 16:32, :].rearrange("p (t c) k -> p t c k", t=HALVES)
        late = sb("late", [P, HEADS, P])
        b_o_row = late[:, 0:KC, :].rearrange("p c k -> p (c k)")
        scores = [late, scores_1]
        qk_gain = sb("qk_gain", [P, 2, HD])
        qk_sum = sb("qk_sum", [P, ITEMS, Q_HEADS])
        qk_mean = sb("qk_mean", [P, ITEMS, Q_HEADS])
        qk_rstd = sb("qk_rstd", [P, ITEMS, Q_HEADS])
        sink_row = sb("sink_row", [P, HEADS])
        soft = sb("soft", [P, HALVES, 7, HEADS])
        MAX, NEG_MAX, SINK, SINK_EXP, SUM, DENOM, RECIP = range(7)

        into = [ctx.enter_context(nc.psum_tensor(f"into{i}", [P, 512], F32)) for i in range(2)]
        turn = [ctx.enter_context(nc.psum_tensor(f"turn{i}", [P, 512], F32)) for i in range(2)]
        accum = [ctx.enter_context(nc.psum_tensor(f"accum{i}", [P, D], F32)) for i in range(2)]

        raw_landed = [sem(f"raw_landed{s}") for s in range(RING)]
        hi_made = sem("hi_made")
        lo_made = sem("lo_made")
        unit_used = sem("unit_used")
        in_done = sem("in_done")
        gate_done = sem("gate_done")
        in_read = sem("in_read")
        turned = sem("turned")
        turn_hi = sem("turn_hi")
        turn_read = sem("turn_read")
        acc_done = sem("acc_done")
        acc_read = sem("acc_read")
        scaled = sem("scaled")
        meansq_done = sem("meansq_done")
        eps_added = sem("eps_added")
        rstd_done = sem("rstd_done")
        vec_step = sem("vec_step")
        x_loaded = [sem(f"x_loaded{t}") for t in range(HALVES)]
        ident_loaded = sem("ident_loaded")
        taps_loaded = sem("taps_loaded")
        gain_loaded = [sem(f"gain_loaded{i}") for i in range(2)]
        gain_loaded_first = sem("gain_loaded_first")
        pool_loaded = sem("pool_loaded")
        attn_loaded = sem("attn_loaded")
        rel_loaded = sem("rel_loaded")
        rel_turned = sem("rel_turned")
        rel_masked = sem("rel_masked")
        rel_stored = sem("rel_stored")
        rel_spread = sem("rel_spread")
        constants = sem("constants")
        product_done = sem("product_done")
        product_hi = sem("product_hi")
        product_split = sem("product_split")
        squared = sem("squared")
        qk_mean_done = sem("qk_mean_done")
        qk_rstd_done = sem("qk_rstd_done")
        q_ready = sem("q_ready")
        max_done = sem("max_done")
        sink_done = sem("sink_done")
        exp_done = sem("exp_done")
        stored = sem("stored")

        def bank(b, chunks):
            return turn[b][:, 0:chunks * P].rearrange("p (c k) -> p c k", c=chunks)

        block = ctx.enter_context(nc.Block())

        @block.sync
        def _(sp):
            def load_unit(n, s, wait):
                if wait is not None:
                    sp.wait_ge(lo_made, wait)
                sp.dma_start(raw[:, s, :], stream[n]).then_inc(raw_landed[s], 16)

            sp.dma_start(x[:, 0, :], x_in[0:P, :]).then_inc(x_loaded[0], 16)
            load_unit(0, 0, None)
            load_unit(1, 1, None)
            sp.dma_start(x[:, 1, :], x_in[P:SEQ, :]).then_inc(x_loaded[1], 16)
            for s in range(2, RING):
                load_unit(s, s, None)
            with sp.Fori(1, units_total // RING) as i:
                for s in range(RING):
                    load_unit(i * RING + s, s, i * RING + (s + 1 - RING))
            sp.wait_ge(stored, 16 * 2 * HALVES)

        @block.gpsimd
        def _(pool):
            def row(ap):
                return ap.partition_broadcast(P)

            def power(to, of, at):
                return pool.tensor_tensor(to, of, neg_half[:, 0:at], ALU.pow)

            pool.memset(neg_half[:, :], -0.5).then_inc(constants, 1)
            pool.dma_start(tap[:, :, :, :], taps).then_inc(taps_loaded, 16)
            pool.dma_start(gain[:, 1, :], row(gains[1])).then_inc(gain_loaded[1], 16)
            pool.dma_start(qk_gain[:, 0, :], row(q_gain)).then_inc(attn_loaded, 16)
            pool.dma_start(qk_gain[:, 1, :], row(k_gain)).then_inc(attn_loaded, 16)
            pool.dma_start(sink_row[:, :], row(sinks)).then_inc(attn_loaded, 16)
            pool.dma_start(b_o_row, row(b_o)).then_inc(attn_loaded, 16)
            pool.wait_ge(constants, 1)
            for ph in phases:
                for t in range(HALVES):
                    n = 2 * ph.index + t + 1
                    pool.wait_ge(meansq_done, n)
                    pool.tensor_scalar(padded[:, t:t + 1], meansq[:, t:t + 1], 1.0, EPS, ALU.mult,
                                       ALU.add).then_inc(eps_added, 1)
                    pool.wait_ge(eps_added, n)
                    power(rstd[:, t:t + 1], padded[:, t:t + 1], 1).then_inc(rstd_done, 1)
                if ph.index and ph.index + 1 < len(phases):
                    i = (ph.index + 1) % 2
                    pool.wait_ge(scaled, 4 * ph.index)
                    pool.dma_start(gain[:, i, :], row(gains[ph.index + 1])).then_inc(gain_loaded[i], 16)
                if ph.index and phases[ph.index - 1].kind == CONV and ph.layer == 0:
                    pool.wait_ge(product_split, CV_TILES)
                    pool.dma_start(averaging, band_in).then_inc(pool_loaded, 16)
                    pool.dma_start(pool_rows[:, 0, :], row(pool_b)).then_inc(pool_loaded, 16)
                    pool.dma_start(pool_rows[:, 1, :], row(pool_scale)).then_inc(pool_loaded, 16)
                    pool.dma_start(onehot, onehot_in).then_inc(rel_loaded, 16)
                    pool.dma_start(rel_in, rel_bias).then_inc(rel_loaded, 16)
                    pool.dma_start(mask_rows, mask_in).then_inc(rel_loaded, 16)
                if ph.index and phases[ph.index - 1].kind == POOL:
                    pool.wait_ge(rel_masked, 1)
                    pool.dma_start(table, rel_rows).then_inc(rel_stored, 16)
                    pool.wait_ge(rel_stored, 16)
                    pool.dma_start(spread.rearrange("q (h k) -> h q k", h=HEADS),
                                   bass.AP(table.tensor, P - 1, [[BAND, HEADS], [-1, P], [1, SEQ]])
                                   ).then_inc(rel_stored, 16)
                    pool.wait_ge(rel_stored, 32)
                    pool.wait_ge(acc_read, 2 * ph.acc)
                    pool.dma_start(rel.rearrange("p h k -> p (h k)"), spread).then_inc(rel_spread, 16)
                    pool.dma_start(bias_qkv[:, 0, :], row(b_qkv)).then_inc(attn_loaded, 16)
                if ph.kind == ATTN:
                    for i in range(ITEMS):
                        n = Q_HEADS if i >= 2 else KV_HEADS
                        pool.wait_ge(qk_mean_done, i + 1)
                        power(qk_rstd[:, i, 0:n], qk_mean[:, i, 0:n], n).then_inc(qk_rstd_done, 1)

        @block.tensor
        def _(pe):
            def release_here(ins, yes):
                if yes:
                    ins.then_inc(unit_used, 1)

            def in_half(ph, i, t, unit, slots, cols=512, units=IN_UNITS, release=False, first_tile=False):
                h = ph.into + i * 2 + t
                if not (isinstance(h, int) and h < 2):
                    pe.wait_ge(in_read, h - 1)
                per = KC // units
                for u in range(units):
                    s = slots[u]
                    for k in range(per):
                        c = u * per + k
                        if t == 0 and k == 0:
                            pe.wait_ge(hi_made, unit + (u + 1))
                        if first_tile and c % 4 == 0:
                            pe.wait_ge(turn_read, ph.norm_fill + 2 * t + c // 4 + 1)
                        wh = w_hi[:, s, k * cols:(k + 1) * cols]
                        wl = w_lo[:, s, k * cols:(k + 1) * cols]
                        o = into[t][:, 0:cols]
                        m = pe.matmul(o, h_hi[:, t, c, :], wh, start=(c == 0), stop=False)
                        release_here(m, release and c == 0)
                        pe.matmul(o, h_lo[:, t, c, :], wh, start=False, stop=False)
                        if t == 0 and k == 0:
                            pe.wait_ge(lo_made, unit + (u + 1))
                        last = pe.matmul(o, h_hi[:, t, c, :], wl, start=False, stop=(c == KC - 1))
                    if t == 1 and u < units - 1:
                        last.then_inc(unit_used, 1)
                last.then_inc(in_done, 1)

            def turn_half(fill, b, source, chunks, ready, release=False):
                if ready is not None:
                    pe.wait_ge(*ready)
                if not (isinstance(fill, int) and fill < 2):
                    pe.wait_ge(turn_read, fill - 1)
                for c in range(chunks):
                    last = pe.transpose(turn[b][:, c * P:(c + 1) * P], source[:, c * P:(c + 1) * P],
                                        ident[:, :])
                    release_here(last, release and c == 0)
                last.then_inc(turned, 1)

            def norm_turns(ph, t):
                if ph is None or ph.kind == POOL:
                    return
                for q in range(2):
                    turn_half(ph.norm_fill + 2 * t + q, q, xn[:, t, q * 512:(q + 1) * 512], 4,
                              (scaled, 4 * ph.index + 2 * t + q + 1))

            def out_unit(t, unit, s, k, start, stop, release=False):
                if t == 0:
                    pe.wait_ge(lo_made, unit + 1)
                for n, (stat, w) in enumerate(((u_hi, w_hi), (u_lo, w_hi), (u_hi, w_lo))):
                    for half in range(2):
                        cols = slice(half * 512, half * 512 + 512)
                        last = pe.matmul(accum[t][:, cols], stat[:, t, k, :], w[:, s, cols],
                                         start=(start and n == 0), stop=(stop and n == 2))
                        release_here(last, release and n == 0 and half == 0)
                return last

            def acc_free(acc):
                if acc >= 2:
                    pe.wait_ge(acc_read, 2 * (acc - 1))

            def out_blocks(ph, nxt, unit, acc, ready, between, release):
                for t, k0, k1 in ((0, 0, 4), (1, 0, 4), (0, 4, KC), (1, 4, 6), (1, 6, KC)):
                    if k0 == 0:
                        acc_free(acc + t)
                    for k in range(k0, k1):
                        ready(t, k)
                        n = unit + k
                        last = out_unit(t, n, n % RING, k, k == 0, k == KC - 1,
                                        release and t == 0 and k == 0)
                        if k == KC - 1:
                            last.then_inc(acc_done, 1)
                        elif t == 1:
                            last.then_inc(unit_used, 1)
                        if t == 0 and k == 1:
                            between()
                    if (t, k1) == (1, 6):
                        norm_turns(nxt, 0)

            def ffn(ph, nxt):
                def in_tile(j, t, first=False, release=False):
                    unit = ph.unit if first else ph.unit + IN_UNITS + (j - 1) * RING
                    at = 0 if first else IN_UNITS
                    in_half(ph, j, t, unit, [(ph.unit + at + u) % RING for u in range(IN_UNITS)],
                            release=release, first_tile=first)

                def turns(j, t):
                    turn_half(ph.fill + (j * 2 + t), t, act[:, t, :], 2, (in_read, ph.into + (j * 2 + (t + 1))))

                def down(j, t, first=False, last=False, release=False):
                    at = 2 * IN_UNITS if not last else FFN_UNITS - OUT_UNITS
                    unit = ph.unit + 2 * IN_UNITS + j * RING if not last else ph.unit + at
                    if first:
                        acc_free(ph.acc + t)
                    pe.wait_ge(turn_read, ph.fill + (j * 2 + (t + 1)))
                    for k in range(OUT_UNITS):
                        end = last and k == OUT_UNITS - 1
                        m = out_unit(t, unit + k, (ph.unit + at + k) % RING, k + (2 if last else 0),
                                     first and k == 0, end, release and k == 0)
                        if end:
                            m.then_inc(acc_done, 1)
                        elif t == 1:
                            m.then_inc(unit_used, 1)

                def tile(j, first=False):
                    in_tile(j, 0, release=first)
                    turns(j - 1, 0)
                    turns(j - 1, 1)
                    in_tile(j, 1)
                    down(j - 1, 0, first=first, release=True)
                    down(j - 1, 1, first=first)

                end = FTILES - 1
                in_tile(0, 0, first=True, release=ph.index > 0)
                norm_turns(ph, 1)
                in_tile(0, 1, first=True)
                tile(1, first=True)
                with pe.Fori(2, end) as j:
                    tile(j)
                in_tile(end, 0)
                turns(end - 1, 0)
                turns(end - 1, 1)
                in_tile(end, 1)
                down(end - 1, 0, release=True)
                turns(end, 0)
                turns(end, 1)
                down(end, 0, last=True)
                down(end - 1, 1)
                norm_turns(nxt, 0)
                down(end, 1, last=True)

            def conv_mixer(ph, nxt):
                def turns(i, t):
                    rows_of = b_rows if i < B_TILES else act
                    turn_half(ph.fill + 2 * i + t, t, rows_of[:, t, :], 4 if i < B_TILES else 2,
                              (in_read, ph.into + 2 * i + t + 1), t == 0 and i < CONV_TILES - 1)

                for i in range(CONV_TILES):
                    unit = ph.unit + IN_UNITS * i
                    slots = [(unit + u) % RING for u in range(IN_UNITS)]
                    in_half(ph, i, 0, unit, slots, release=(i == 0), first_tile=(i == 0))
                    norm_turns(ph, 1) if i == 0 else turns(i - 1, 1)
                    in_half(ph, i, 1, unit, slots, first_tile=(i == 0))
                    turns(i, 0)
                base = CV_TILES * ph.nth

                def ready(t, k):
                    if k % 2 == 0:
                        pe.wait_ge(product_split, base + k // 2 + 1)

                out_blocks(ph, nxt, ph.unit + CONV_TILES * IN_UNITS, ph.acc, ready,
                           lambda: turns(CONV_TILES - 1, 1), release=True)

            def pool_mixer(ph, nxt):
                pe.wait_ge(pool_loaded, 48)
                pe.wait_ge(scaled, 4 * ph.index + 4)
                for q in range(4):
                    pe.wait_ge(turn_read, ph.norm_fill + q - 1)
                    for k in range(2):
                        c = 2 * q + k
                        cols = slice(c * P, (c + 1) * P)
                        m = pe.matmul(turn[q % 2][:, k * SEQ:(k + 1) * SEQ], xn[:, 0, cols],
                                      averaging[:, q, 0, :], start=True, stop=False)
                        release_here(m, c == 0)
                        last = pe.matmul(turn[q % 2][:, k * SEQ + P:(k + 1) * SEQ], xn[:, 1, cols],
                                         averaging[:, q, 1, P:SEQ], start=False, stop=True)
                    last.then_inc(turned, 1)
                pe.wait_ge(rel_loaded, 48)
                acc_free(ph.acc)
                pe.matmul(accum[0][0:HEADS, 0:BAND], rel_in, onehot, start=True,
                          stop=True).then_inc(rel_turned, 1)
                pe.wait_ge(rel_masked, 1)
                for t in range(HALVES):
                    acc_free(ph.acc + t)
                    for g in range(4):
                        if t == 0:
                            pe.wait_ge(turn_read, ph.norm_fill + g + 1)
                            pe.wait_ge(lo_made, ph.unit + g // 2 + 1)
                        s = (ph.unit + g // 2) % RING
                        o = accum[t][:, g * FT:(g + 1) * FT]
                        for k in range(2):
                            c = 2 * g + k
                            cols = slice(((g % 2) * 2 + k) * FT, ((g % 2) * 2 + k + 1) * FT)
                            pe.matmul(o, h_hi[:, t, c, :], w_hi[:, s, cols], start=(k == 0), stop=False)
                            pe.matmul(o, h_lo[:, t, c, :], w_hi[:, s, cols], start=False, stop=False)
                            last = pe.matmul(o, h_hi[:, t, c, :], w_lo[:, s, cols], start=False,
                                             stop=(k == 1))
                        if t == 1 and g == 1:
                            last.then_inc(unit_used, 1)
                    last.then_inc(acc_done, 1)
                norm_turns(nxt, 0)

            def attn_mixer(ph, nxt):
                fill = [ph.fill]
                score = [ph.into + ITEMS]

                def item_turn(i, release=False):
                    t = i % 2
                    if i < 2:
                        source, chunks = k_twice.rearrange("p a b -> p (a b)"), 2
                    else:
                        source, chunks = xn[:, t, (i // 2 - 1) * 512:(i // 2) * 512], 4
                    turn_half(fill[0], fill[0] % 2, source, chunks, (q_ready, i + 1), release)
                    fill[0] += 1

                def score_fills(t):
                    keys = (t + 1) * P
                    for b in range(HEADS // 2):
                        h = score[0]
                        pe.wait_ge(in_read, h - 1)
                        if t == 0 and b in (0, 4):
                            pe.wait_ge(turn_read, ph.fill + (3 if b == 0 else 5))
                        odd = b % 2
                        for m in range(2):
                            head = 4 * (b // 2) + 2 * m + odd
                            last = pe.matmul(into[h % 2][:, m * SEQ:m * SEQ + keys],
                                             q_t[odd * HD:(odd + 1) * HD, t, head // 2, :],
                                             k_t[odd * HD:(odd + 1) * HD, head // 8, 0:keys],
                                             start=True, stop=True)
                        last.then_inc(in_done, 1)
                        score[0] += 1

                def blocks(t):
                    return [(head, kb) for head in range(HEADS) for kb in range(t + 1)]

                def prob_turns(t):
                    for g in range(4 * (t + 1)):
                        four = blocks(t)[4 * g:4 * g + 4]
                        pe.wait_ge(exp_done, t * HEADS + four[-1][0] + 1)
                        pe.wait_ge(turn_read, fill[0] - 1)
                        for m, (head, kb) in enumerate(four):
                            last = pe.transpose(turn[fill[0] % 2][:, m * P:(m + 1) * P],
                                                scores[t][:, head, kb * P:(kb + 1) * P], ident[:, :])
                        last.then_inc(turned, 1)
                        fill[0] += 1

                def values(t):
                    pe.wait_ge(turn_read, ph.fill + 6 + 4 * (1 + 2 * t))
                    acc_free(ph.acc + t)
                    for n, (head, kb) in enumerate(blocks(t)):
                        at = NQK * HD + (head // 8) * HD
                        last = pe.matmul(accum[t][:, head * HD:(head + 1) * HD], probs_t[:, n, :],
                                         qkv[:, kb, at:at + HD], start=(kb == 0), stop=(kb == t))
                    last.then_inc(acc_done, 1)

                def output_turns(t):
                    for q in range(2):
                        turn_half(fill[0], fill[0] % 2, xn[:, t, q * 512:(q + 1) * 512], 4,
                                  (acc_read, 2 * (ph.acc + t) + q + 1))
                        fill[0] += 1

                tiles = ((ph.unit, KV_UNITS, 256), (ph.unit + KV_UNITS, IN_UNITS, 512),
                         (ph.unit + KV_UNITS + IN_UNITS, IN_UNITS, 512))
                for i, (unit, units, cols) in enumerate(tiles):
                    slots = [(unit + u) % RING for u in range(units)]
                    in_half(ph, i, 0, unit, slots, cols, units, release=True, first_tile=(i == 0))
                    norm_turns(ph, 1) if i == 0 else item_turn(2 * i - 2)
                    in_half(ph, i, 1, unit, slots, cols, units, first_tile=(i == 0))
                    if i:
                        item_turn(2 * i - 1, release=(i == 2))
                item_turn(4)
                score_fills(0)
                item_turn(5)
                pe.wait_ge(turn_read, ph.fill + 6)
                score_fills(1)
                prob_turns(0)
                values(0)
                prob_turns(1)
                output_turns(0)
                values(1)

                def ready(t, k):
                    if k % 4 == 0:
                        pe.wait_ge(turn_read, ph.fill + FILLS[ATTN] - 4 + 2 * t + k // 4 + 1)

                def between():
                    output_turns(1)

                out_blocks(ph, nxt, ph.unit + KV_UNITS + 2 * IN_UNITS, ph.acc + 2, ready, between,
                           release=False)
                assert fill[0] == ph.fill + FILLS[ATTN]

            pe.wait_ge(ident_loaded, 16)
            norm_turns(phases[0], 0)
            for ph, nxt in zip(phases, phases[1:] + [None]):
                {FFN: ffn, CONV: conv_mixer, POOL: pool_mixer, ATTN: attn_mixer}[ph.kind](ph, nxt)

        @block.scalar
        def _(sc):
            def hi_unit(s, landed, wait):
                sc.wait_ge(raw_landed[s], landed)
                if wait is not None:
                    sc.wait_ge(unit_used, wait)
                sc.activation(w_hi[:, s, :], raw[:, s, :], ACT.Copy).then_inc(hi_made, 1)

            def hi_units(n0, n1):
                for n in range(n0, n1):
                    hi_unit(n % RING, 16 * (n // RING + 1), n - RING + 1 if n >= RING else None)

            def turn_split(b, to, f):
                sc.wait_ge(turned, f)
                sc.activation(to, bank(b, to.shape[1]), ACT.Copy).then_inc(turn_hi, 1)

            def mean_square(ph, t):
                if ph.index:
                    sc.wait_ge(acc_read, 2 * (ph.acc - 1 + t))
                else:
                    sc.wait_ge(x_loaded[t], 16)
                sc.activation(squares[:, t, :], x[:, t, :], ACT.Square, scale=D ** -0.5,
                              accum_out=meansq[:, t:t + 1]).then_inc(meansq_done, 1)

            def boundary(ph, early):
                late_units = (early, min(ph.unit + IN_UNITS, units_total))
                for t in range(HALVES):
                    if ph.kind == POOL:
                        mean_square(ph, t)
                    else:
                        for q in range(2):
                            turn_split(q, h_hi[:, t, 4 * q:4 * q + 4, :], ph.norm_fill + 2 * t + q + 1)
                        mean_square(ph, t)
                    if t == 0:
                        hi_units(*late_units)
                sc.wait_ge(rstd_done, 2 * ph.index + 2)

            def gate(ph, i, t, func):
                sc.wait_ge(in_done, ph.into + (i * 2 + (t + 1)))
                sc.activation(gated[:, t, :], into[t][:, 0:FT], func,
                              scale=rstd[:, t:t + 1]).then_inc(gate_done, 1)

            def ffn(ph):
                def ahead(j, a, b):
                    for u in range(a, b):
                        at = ph.unit + IN_UNITS + u
                        if isinstance(j, int):
                            hi_units(at + RING * j, at + RING * j + 1)
                        else:
                            hi_unit(at % RING, (j + (at // RING + 1)) * 16, j * RING + (at - RING + 1))

                def split(j, t, k=0):
                    turn_split(t, u_hi[:, t, k:k + 2, :], ph.fill + (j * 2 + (t + 1)))

                def tile(j, first=False):
                    gate(ph, j, 0, ACT.Silu)
                    if not first:
                        split(j - 1, 0)
                        split(j - 1, 1)
                    ahead(j, 0, IN_UNITS)
                    gate(ph, j, 1, ACT.Silu)
                    ahead(j, IN_UNITS, RING)

                end = FTILES - 1
                tile(0, first=True)
                with sc.Fori(1, end) as j:
                    tile(j)
                gate(ph, end, 0, ACT.Silu)
                split(end - 1, 0)
                split(end - 1, 1)
                gate(ph, end, 1, ACT.Silu)
                hi_units(ph.next_unit - OUT_UNITS, ph.next_unit)
                for t in range(HALVES):
                    split(end, t, 2)
                return min(ph.next_unit + 2, units_total)

            def conv_mixer(ph):
                out0 = ph.unit + CONV_TILES * IN_UNITS

                def product_split_hi(m):
                    sc.wait_ge(product_done, CV_TILES * ph.nth + m + 1)
                    sc.activation(u_hi[:, :, 2 * m:2 * m + 2, :].rearrange("p t c k -> p c t k"),
                                  product.rearrange("p c (t k) -> p c t k", t=HALVES),
                                  ACT.Copy).then_inc(product_hi, 1)

                for i in range(CONV_TILES):
                    nxt = ph.unit + IN_UNITS * (i + 1)
                    if i >= B_TILES:
                        gate(ph, i, 0, ACT.Copy)
                    hi_units(nxt, nxt + IN_UNITS)
                    if i > B_TILES:
                        product_split_hi(i - 1 - B_TILES)
                    if i >= B_TILES:
                        gate(ph, i, 1, ACT.Copy)
                hi_units(out0 + 4, out0 + 6)
                product_split_hi(CV_TILES - 1)
                hi_units(out0 + 6, out0 + KC)
                return ph.next_unit

            def pool_mixer(ph):
                for q in range(4):
                    sc.wait_ge(turned, ph.norm_fill + q + 1)
                    sc.activation(h_hi[:, :, 2 * q:2 * q + 2, :].rearrange("p t c k -> p c t k"),
                                  turn[q % 2][:, :].rearrange("p (c t k) -> p c t k", c=2, t=2),
                                  ACT.Copy).then_inc(turn_hi, 1)
                return ph.unit + IN_UNITS

            def attn_mixer(ph):
                q0 = ph.unit + KV_UNITS
                out0 = q0 + 2 * IN_UNITS

                def square(i):
                    t = i % 2
                    cols = slice(D, D + P) if i < 2 else slice((i // 2 - 1) * 512, (i // 2) * 512)
                    n = P if i < 2 else 512
                    sc.wait_ge(in_read, ph.into + i + 1)
                    if i >= 2:
                        sc.wait_ge(qk_mean_done, i - 1)
                    sc.activation(qk_sq[:, i % 2, 0:n], qkv[:, t, cols], ACT.Square,
                                  scale=HD ** -0.5).then_inc(squared, 1)

                square(0)
                hi_units(q0 + 2, q0 + 4)
                square(1)
                square(2)
                hi_units(q0 + 4, q0 + 8)
                square(3)
                square(4)
                hi_units(out0, out0 + 4)
                square(5)
                hi_units(out0 + 4, out0 + 6)
                for t in range(HALVES):
                    sc.wait_ge(max_done, t + 1)
                    sc.activation(soft[:, t, SINK_EXP, :], soft[:, t, SINK, :], ACT.Exp).then_inc(sink_done, 1)
                    for head in range(HEADS):
                        keys = scores[t][:, head, 0:(t + 1) * P]
                        sc.activation(keys, keys, ACT.Exp, bias=soft[:, t, NEG_MAX, head:head + 1],
                                      accum_out=soft[:, t, SUM, head:head + 1]).then_inc(exp_done, 1)
                f = ph.fill + FILLS[ATTN] - 4
                for t in range(HALVES):
                    for q in range(2):
                        f += 1
                        turn_split((f - 1) % 2, u_hi[:, t, 4 * q:4 * q + 4, :], f)
                hi_units(out0 + 6, out0 + KC)
                return ph.next_unit

            sc.dma_start(gain[:, 0, :], gains[0].partition_broadcast(P)).then_inc(gain_loaded_first, 16)
            sc.dma_start(ident[:, :], ident_in).then_inc(ident_loaded, 16)
            early = 0
            for ph in phases:
                boundary(ph, early)
                early = {FFN: ffn, CONV: conv_mixer, POOL: pool_mixer, ATTN: attn_mixer}[ph.kind](ph)
                if ph.kind == FFN:
                    hi_units(ph.next_unit, early)
            acc = phases[-1].acc
            for t in range(HALVES):
                for q in range(2):
                    cols = slice(q * 512, (q + 1) * 512)
                    sc.wait_ge(acc_read, 2 * (acc + t) + q + 1)
                    sc.dma_start(out[t * P:(t + 1) * P, cols], x[:, t, cols]).then_inc(stored, 16)

        @block.vector
        def _(ve):
            steps = [0]
            turn_his = [0]
            gates = [0]

            def step(ins):
                steps[0] += 1
                ins.then_inc(vec_step, 1)

            def settle():
                ve.wait_ge(vec_step, steps[0])

            def link(ins):
                step(ins)
                settle()

            def lo_unit(s, made):
                ve.wait_ge(hi_made, made)
                ve.tensor_tensor(w_lo[:, s, :], raw[:, s, :], w_hi[:, s, :].bitcast(F32),
                                 ALU.subtract).then_inc(lo_made, 1)

            def lo_units(n0, n1):
                for n in range(n0, n1):
                    lo_unit(n % RING, n + 1)

            def turn_split(b, to, hi, count):
                ve.wait_ge(turn_hi, count)
                ve.tensor_tensor(to, bank(b, to.shape[1]), hi.bitcast(F32),
                                 ALU.subtract).then_inc(turn_read, 1)

            def residual(ph, t, q):
                cols = slice(q * 512, (q + 1) * 512)
                if q == 0:
                    ve.wait_ge(acc_done, ph.acc + (2 if ph.kind == ATTN else 0) + t + 1)
                if ph.kind == POOL:
                    y = pool_y[:, t, cols]
                    link(ve.tensor_tensor(y, accum[t][:, cols], pool_rows[:, 0, cols], ALU.add))
                    link(ve.tensor_tensor(y, y, pool_rows[:, 1, cols], ALU.mult))
                    ins = ve.tensor_tensor(x[:, t, cols], y, x[:, t, cols], ALU.add)
                else:
                    ins = ve.scalar_tensor_tensor(out=x[:, t, cols], in0=accum[t][:, cols],
                                                  scalar=0.5 if ph.kind == FFN else 1.0,
                                                  in1=x[:, t, cols], op0=ALU.mult, op1=ALU.add)
                ins.then_inc(acc_read, 1)

            def boundary(prev, ph, early):
                def scale(t, q):
                    g = ph.index % 2
                    cols = slice(q * 512, (q + 1) * 512)
                    if ph.kind == POOL:
                        ve.scalar_tensor_tensor(out=xn[:, t, cols], in0=x[:, t, cols],
                                                scalar=rstd[:, t:t + 1], in1=gain[:, g, cols],
                                                op0=ALU.mult, op1=ALU.mult).then_inc(scaled, 1)
                    else:
                        ve.tensor_tensor(xn[:, t, cols], x[:, t, cols], gain[:, g, cols],
                                         ALU.mult).then_inc(scaled, 1)

                if ph.index == 0:
                    ve.wait_ge(gain_loaded_first, 16)
                else:
                    ve.wait_ge(gain_loaded[ph.index % 2], 16 * ((ph.index + 1) // 2))
                for t in range(HALVES):
                    if prev is None:
                        ve.wait_ge(x_loaded[t], 16)
                    for q in range(2):
                        if prev is not None:
                            residual(prev, t, q)
                        if ph.kind != POOL:
                            if prev is not None:
                                ve.wait_ge(acc_read, 2 * (ph.acc - 2 + t) + q + 1)
                            scale(t, q)
                    if ph.kind == POOL:
                        if t == 0:
                            lo_units(early, min(ph.unit + IN_UNITS, units_total))
                        continue
                    for q in range(2):
                        turn_his[0] += 1
                        turn_split(q, h_lo[:, t, 4 * q:4 * q + 4, :], h_hi[:, t, 4 * q:4 * q + 4, :],
                                   turn_his[0])
                    if t == 0:
                        lo_units(early, min(ph.unit + IN_UNITS, units_total))
                ve.wait_ge(rstd_done, 2 * ph.index + 2)
                if ph.kind == POOL:
                    for t in range(HALVES):
                        for q in range(2):
                            scale(t, q)

            def times(ph, i, t):
                ve.wait_ge(gate_done, gates[0] + (i * 2 + (t + 1)))
                ve.scalar_tensor_tensor(out=act[:, t, :], in0=into[t][:, FT:2 * FT], scalar=rstd[:, t:t + 1],
                                        in1=gated[:, t, :], op0=ALU.mult, op1=ALU.mult).then_inc(in_read, 1)

            def ffn(ph):
                his = turn_his[0]

                def ahead(j, a, b):
                    for u in range(a, b):
                        at = ph.unit + IN_UNITS + u
                        lo_unit(at % RING, j * RING + (at + 1))

                def split(j, t, k=0):
                    turn_split(t, u_lo[:, t, k:k + 2, :], u_hi[:, t, k:k + 2, :], his + (j * 2 + (t + 1)))

                def product_of(j, t, first=False):
                    if not first:
                        ve.wait_ge(turned, ph.fill + ((j - 1) * 2 + (t + 1)))
                    times(ph, j, t)

                def tile(j, first=False):
                    product_of(j, 0, first)
                    if not first:
                        split(j - 1, 0)
                        split(j - 1, 1)
                    ahead(j, 0, IN_UNITS)
                    product_of(j, 1, first)
                    ahead(j, IN_UNITS, RING)

                end = FTILES - 1
                tile(0, first=True)
                with ve.Fori(1, end) as j:
                    tile(j)
                product_of(end, 0)
                split(end - 1, 0)
                split(end - 1, 1)
                product_of(end, 1)
                lo_units(ph.next_unit - OUT_UNITS, ph.next_unit)
                for t in range(HALVES):
                    split(end, t, 2)
                gates[0] += 2 * FTILES
                turn_his[0] += 2 * FTILES
                return min(ph.next_unit + 2, units_total)

            def conv_mixer(ph):
                out0 = ph.unit + CONV_TILES * IN_UNITS
                base = CV_TILES * ph.nth

                def b_turned(i, t):
                    ve.wait_ge(turned, ph.fill + 2 * i + t + 1)
                    ve.tensor_copy(b_t[:, 4 * i:4 * i + 4, t * P:(t + 1) * P],
                                   bank(t, 4)).then_inc(turn_read, 1)

                def z_turned(i, t):
                    m = i - B_TILES
                    ve.wait_ge(turned, ph.fill + 2 * i + t + 1)
                    a = TAPS - 1 + t * P
                    ve.tensor_copy(z_t[:, 2 * m:2 * m + 2, a:a + P], bank(t, 2)).then_inc(turn_read, 1)

                def convolve(m):
                    ve.wait_ge(turn_read, ph.fill + 2 * (m + B_TILES) + 2)
                    for tp in range(TAPS):
                        for c in range(2):
                            z = z_t[:, 2 * m + c, tp:tp + SEQ]
                            o = product[:, c, :]
                            w = tap[:, ph.nth, tp, 2 * m + c:2 * m + c + 1]
                            if tp == 0:
                                step(ve.tensor_scalar(o, z, w, None, ALU.mult))
                            else:
                                step(ve.scalar_tensor_tensor(out=o, in0=z, scalar=w, in1=o,
                                                             op0=ALU.mult, op1=ALU.add))
                        settle()
                    ve.tensor_tensor(product, product, b_t[:, 2 * m:2 * m + 2, :],
                                     ALU.mult).then_inc(product_done, 1)

                def product_lo(m):
                    ve.wait_ge(product_hi, base + m + 1)
                    chunks = slice(2 * m, 2 * m + 2)
                    ve.tensor_tensor(u_lo[:, :, chunks, :].rearrange("p t c k -> p c t k"),
                                     product.rearrange("p c (t k) -> p c t k", t=HALVES),
                                     u_hi[:, :, chunks, :].rearrange("p t c k -> p c t k").bitcast(F32),
                                     ALU.subtract).then_inc(product_split, 1)

                link(ve.memset(z_t[:, :, 0:TAPS - 1], 0.0))
                ve.wait_ge(taps_loaded, 16)
                for i in range(CONV_TILES):
                    nxt = ph.unit + IN_UNITS * (i + 1)
                    for t in range(HALVES):
                        if i < B_TILES:
                            ve.wait_ge(in_done, ph.into + 2 * i + t + 1)
                            ve.tensor_scalar(b_rows[:, t, :], into[t][:, :], rstd[:, t:t + 1], None,
                                             ALU.mult).then_inc(in_read, 1)
                        else:
                            times(ph, i - B_TILES, t)
                        if t == 0:
                            if 0 < i <= B_TILES:
                                b_turned(i - 1, 1)
                            elif i > B_TILES:
                                z_turned(i - 1, 1)
                                convolve(i - 1 - B_TILES)
                            lo_units(nxt, nxt + IN_UNITS)
                            if i > B_TILES:
                                product_lo(i - 1 - B_TILES)
                    b_turned(i, 0) if i < B_TILES else z_turned(i, 0)
                z_turned(CONV_TILES - 1, 1)
                convolve(CV_TILES - 1)
                lo_units(out0 + 4, out0 + 6)
                product_lo(CV_TILES - 1)
                lo_units(out0 + 6, out0 + KC)
                gates[0] += 2 * CV_TILES
                return ph.next_unit

            def pool_mixer(ph):
                for q in range(4):
                    turn_his[0] += 1
                    ve.wait_ge(turn_hi, turn_his[0])
                    chunks = slice(2 * q, 2 * q + 2)
                    ve.tensor_tensor(h_lo[:, :, chunks, :].rearrange("p t c k -> p c t k"),
                                     turn[q % 2][:, :].rearrange("p (c t k) -> p c t k", c=2, t=2),
                                     h_hi[:, :, chunks, :].rearrange("p t c k -> p c t k").bitcast(F32),
                                     ALU.subtract).then_inc(turn_read, 1)
                ve.wait_ge(rel_turned, 1)
                ve.tensor_tensor(rel_rows, accum[0][0:HEADS, 0:BAND], mask_rows, ALU.add).then_inc(rel_masked, 1)
                return ph.unit + IN_UNITS

            def attn_mixer(ph):
                q0 = ph.unit + KV_UNITS
                out0 = q0 + 2 * IN_UNITS

                def cols_of(i):
                    return (slice(D, QKV), slice(D, D + P)) if i < 2 else \
                        (slice((i // 2 - 1) * 512, (i // 2) * 512),) * 2

                def heads_of(i):
                    return KV_HEADS if i < 2 else Q_HEADS

                def item(i):
                    cols = cols_of(i)[0]
                    n = cols.stop - cols.start
                    ve.wait_ge(in_done, ph.into + i + 1)
                    ve.scalar_tensor_tensor(out=qkv[:, i % 2, cols], in0=into[i % 2][:, 0:n],
                                            scalar=rstd[:, i % 2:i % 2 + 1], in1=bias_qkv[:, 0, cols],
                                            op0=ALU.mult, op1=ALU.add).then_inc(in_read, 1)

                def item_mean(i):
                    n = heads_of(i)
                    ve.wait_ge(squared, i + 1)
                    link(ve.tensor_reduce(qk_sum[:, i, 0:n],
                                          qk_sq[:, i % 2, 0:n * HD].rearrange("p (h d) -> p h d", d=HD),
                                          AX.X, ALU.add))
                    ve.tensor_scalar(qk_mean[:, i, 0:n], qk_sum[:, i, 0:n], EPS, None,
                                     ALU.add).then_inc(qk_mean_done, 1)

                def item_norm(i):
                    n, t = heads_of(i), i % 2
                    heads = qkv[:, t, cols_of(i)[1]].rearrange("p (h d) -> p h d", d=HD)
                    ve.wait_ge(qk_rstd_done, i + 1)
                    link(ve.tensor_tensor(heads, heads, qk_rstd[:, i, 0:n].unsqueeze(2).broadcast_to([P, n, HD]),
                                          ALU.mult))
                    if i < 2:
                        if i:
                            ve.wait_ge(turned, ph.fill + 1)
                        for a in range(2):
                            ins = ve.tensor_tensor(
                                k_twice.rearrange("p h (a d) -> p h a d", a=2)[:, :, a, :], heads,
                                qk_gain[:, 1, :].unsqueeze(1).broadcast_to([P, n, HD]), ALU.mult)
                            if a == 0:
                                step(ins)
                    else:
                        rows_of = xn[:, t, (i // 2 - 1) * 512:(i // 2) * 512]
                        ins = ve.tensor_tensor(rows_of.rearrange("p (h d) -> p h d", d=HD), heads,
                                               qk_gain[:, 0, :].unsqueeze(1).broadcast_to([P, n, HD]),
                                               ALU.mult)
                    ins.then_inc(q_ready, 1)

                def item_turned(i):
                    t, f = i % 2, ph.fill + i
                    ve.wait_ge(turned, f + 1)
                    if i < 2:
                        to, chunks = k_t[:, :, t * P:(t + 1) * P], 2
                    else:
                        to, chunks = q_t[:, t, (i // 2 - 1) * 4:(i // 2) * 4, :], 4
                    ve.tensor_copy(to, bank(f % 2, chunks)).then_inc(turn_read, 1)

                def score_fills(t, b0, b1):
                    keys = (t + 1) * P
                    for b in range(b0, b1):
                        h = ph.into + ITEMS + t * (HEADS // 2) + b
                        ve.wait_ge(in_done, h + 1)
                        h0 = 4 * (b // 2) + b % 2
                        ve.scalar_tensor_tensor(
                            out=scores[t][:, h0:h0 + 3:2, 0:keys],
                            in0=into[h % 2][:, :].rearrange("p (a k) -> p a k", a=2)[:, :, 0:keys],
                            scalar=HD ** -0.5, in1=rel[:, h0:h0 + 3:2, SEQ - keys:SEQ],
                            op0=ALU.mult, op1=ALU.add).then_inc(in_read, 1)

                def maximum(t):
                    s = lambda k: soft[:, t, k, :]
                    ve.wait_ge(in_read, ph.into + ITEMS + (t + 1) * (HEADS // 2))
                    link(ve.tensor_reduce(s(MAX), scores[t][:, :, 0:(t + 1) * P], AX.X, ALU.max))
                    link(ve.tensor_tensor(s(MAX), s(MAX), sink_row[:, :], ALU.max))
                    link(ve.tensor_scalar(s(NEG_MAX), s(MAX), -1.0, None, ALU.mult))
                    ve.tensor_tensor(s(SINK), sink_row[:, :], s(NEG_MAX), ALU.add).then_inc(max_done, 1)

                def probs_turned(t):
                    for g in range(4 * (t + 1)):
                        f = ph.fill + ITEMS + 4 * t + g
                        ve.wait_ge(turned, f + 1)
                        if t and g == 0:
                            ve.wait_ge(acc_done, ph.acc + 1)
                        ve.tensor_copy(probs_t[:, 4 * g:4 * g + 4, :], bank(f % 2, 4)).then_inc(turn_read, 1)

                def output(t):
                    s = lambda k: soft[:, t, k, :]
                    ve.wait_ge(sink_done, t + 1)
                    ve.wait_ge(exp_done, HEADS * (t + 1))
                    link(ve.tensor_tensor(s(DENOM), s(SUM), s(SINK_EXP), ALU.add))
                    link(ve.reciprocal(s(RECIP), s(DENOM)))
                    ve.wait_ge(acc_done, ph.acc + t + 1)
                    for q in range(2):
                        cols, n = slice(q * 512, (q + 1) * 512), HEADS // 2
                        ve.tensor_tensor(xn[:, t, cols].rearrange("p (h d) -> p h d", d=HD),
                                         accum[t][:, cols].rearrange("p (h d) -> p h d", d=HD),
                                         soft[:, t, RECIP, q * n:(q + 1) * n].unsqueeze(2).broadcast_to([P, n, HD]),
                                         ALU.mult).then_inc(acc_read, 1)

                def output_split(t):
                    for q in range(2):
                        f = ph.fill + FILLS[ATTN] - 4 + 2 * t + q
                        turn_his[0] += 1
                        turn_split(f % 2, u_lo[:, t, 4 * q:4 * q + 4, :],
                                   u_hi[:, t, 4 * q:4 * q + 4, :], turn_his[0])

                ve.wait_ge(attn_loaded, 16 * 5)
                item(0)
                lo_units(q0 + 2, q0 + 3)
                item_mean(0)
                lo_units(q0 + 3, q0 + 4)
                item(1)
                item_norm(0)
                item_mean(1)
                step(ve.tensor_tensor(x[:, 0, :], x[:, 0, :], b_o_row, ALU.add))
                step(ve.tensor_tensor(x[:, 1, :], x[:, 1, :], b_o_row, ALU.add))
                item(2)
                item_turned(0)
                item_norm(1)
                item_mean(2)
                lo_units(q0 + 4, q0 + 6)
                item_norm(2)
                lo_units(q0 + 6, q0 + 8)
                item(3)
                item_turned(1)
                item_mean(3)
                item(4)
                item_norm(3)
                item_turned(2)
                item_mean(4)
                lo_units(out0, out0 + 2)
                item_norm(4)
                lo_units(out0 + 2, out0 + 4)
                item(5)
                item_turned(3)
                item_turned(4)
                ve.wait_ge(rel_spread, 16)
                item_mean(5)
                score_fills(0, 0, 3)
                item_norm(5)
                score_fills(0, 3, 8)
                settle()
                item_turned(5)
                maximum(0)
                score_fills(1, 0, 8)
                maximum(1)
                lo_units(out0 + 4, out0 + 6)
                probs_turned(0)
                output(0)
                probs_turned(1)
                output_split(0)
                output(1)
                output_split(1)
                lo_units(out0 + 6, out0 + KC)
                return ph.next_unit

            early, prev = 0, None
            for ph in phases:
                boundary(prev, ph, early)
                early = {FFN: ffn, CONV: conv_mixer, POOL: pool_mixer, ATTN: attn_mixer}[ph.kind](ph)
                if ph.kind == FFN:
                    lo_units(ph.next_unit, early)
                prev = ph
            for t in range(HALVES):
                for q in range(2):
                    residual(prev, t, q)


def _buckets():
    import math

    import numpy as np

    dist = 255 - np.arange(BAND)
    inside = (dist >= 0) & (dist < 128)
    n = np.where(inside, dist, 0)
    nf = np.maximum(n, 1).astype(np.float32)
    large = 16 + (np.log(nf / 16) / math.log(128 / 16) * 16).astype(np.int32)
    bucket = np.where(n < 16, n, np.minimum(large, 31)).astype(np.int32)
    onehot = np.zeros((32, BAND), np.float32)
    onehot[bucket[inside], np.nonzero(inside)[0]] = 1.0
    mask = np.where(inside, 0.0, -1e30).astype(np.float32)
    return onehot, np.ascontiguousarray(np.broadcast_to(mask, (HEADS, BAND)))


def _averaging():
    import numpy as np

    m = np.zeros((P, 4, 2, SEQ), np.float32)
    for g, win in enumerate(POOL_WINDOWS):
        for s in range(SEQ):
            for r in range(max(0, s - win + 1), s + 1):
                m[r % P, g, r // P, s] += np.float32(1.0 / min(s + 1, win))
            m[s % P, g, s // P, s] -= 1.0
    return m


def _stream(a):
    import numpy as np

    def wide(w, groups, tiles, width):
        w = w.reshape(-1, UNIT // (groups * width), P, groups, tiles, width)
        return w.transpose(4, 0, 2, 1, 3, 5).reshape(-1, P, UNIT)

    def ffn(w_in, w_out):
        a_in = wide(w_in, 2, FTILES, FT).reshape(FTILES, IN_UNITS, P, UNIT)
        a_out = w_out.reshape(FTILES, OUT_UNITS, P, UNIT)
        parts = [a_in[0]]
        for j in range(1, FTILES):
            parts += [a_in[j], a_out[j - 1]]
        return parts + [a_out[FTILES - 1]]

    def conv(w_in, w_out):
        return [wide(w_in[:, :D], 1, B_TILES, 512), wide(w_in[:, D:], 2, CV_TILES, FT),
                w_out.reshape(KC, P, UNIT)]

    def pool(w):
        return [w.reshape(2, 2, 2, P, FT).transpose(0, 3, 1, 2, 4).reshape(2, P, UNIT)]

    def attn(w_qkv, w_o):
        return [wide(w_qkv[:, D:], 1, 1, 256), wide(w_qkv[:, :D], 1, 2, 512), w_o.reshape(KC, P, UNIT)]

    parts = []
    for layer in range(DEPTH):
        parts += ffn(a["ffn1_w_in"][layer], a["ffn1_w_out"][layer])
        if layer % 3 == 0:
            parts += conv(a["conv_w_in"][layer // 3], a["conv_w_out"][layer // 3])
        elif layer % 3 == 1:
            parts += pool(a["pool_w"][0])
        else:
            parts += attn(a["attn_w_qkv"][0], a["attn_w_o"][0])
        parts += ffn(a["ffn2_w_in"][layer], a["ffn2_w_out"][layer])
    return np.concatenate(parts)


def kernel(**inputs):
    import concourse.bacc as bacc
    import numpy as np
    from concourse.bass_utils import run_bass_kernel_spmd

    a = {k: np.asarray(v) for k, v in inputs.items()}
    onehot, mask = _buckets()
    arrays = {
        "stream": _stream(a),
        "x_in": a["x"].reshape(SEQ, D),
        "gains": np.stack([a["ffn1_norm"], a["mix_norm"], a["ffn2_norm"]], 1).reshape(3 * DEPTH, D),
        "taps": a["conv_w"].reshape(2, TAPS, KC, P).transpose(3, 0, 1, 2),
        "pool_b": a["pool_b"][0],
        "pool_scale": a["pool_scale"][0],
        "b_qkv": a["attn_b_qkv"][0],
        "q_gain": a["attn_q_norm"][0],
        "k_gain": a["attn_k_norm"][0],
        "sinks": a["attn_sinks"][0],
        "b_o": a["attn_b_o"][0],
        "rel_bias": a["rel_bias"],
        "ident_in": np.eye(P, dtype=np.float32),
        "band_in": _averaging(),
        "onehot_in": onehot,
        "mask_in": mask,
    }
    arrays = {k: np.ascontiguousarray(v) for k, v in arrays.items()}
    nc = bacc.Bacc("TRN2", target_bir_lowering=False, num_devices=1)
    args = {k: nc.dram_tensor(k, v.shape, mybir.dt.from_np(v.dtype), kind="ExternalInput").ap()
            for k, v in arrays.items()}
    args["table"] = nc.dram_tensor("table", (HEADS, BAND), F32, kind="Internal").ap()
    args["spread"] = nc.dram_tensor("spread", (P, HEADS * SEQ), F32, kind="Internal").ap()
    args["out"] = nc.dram_tensor("y", (SEQ, D), F32, kind="ExternalOutput").ap()
    build(nc, **args)
    r = run_bass_kernel_spmd(nc, [arrays], core_ids=[0])
    return r.results[0]["y"].reshape(1, SEQ, D)
```

```python
from contextlib import ExitStack

import concourse.bass as bass
from concourse import mybir

F32 = mybir.dt.float32
F32R = mybir.dt.float32r
ALU = mybir.AluOpType
ACT = mybir.ActivationFunctionType
AX = mybir.AxisListType

P = 128
D = 1024
SEQ = 256
DEPTH = 4
DFF = 2816
HALVES = SEQ // P
KC = D // P
UNIT = 1024
RING = 6
FT = 256
FTILES = DFF // FT
IN_UNITS = KC * 2 * FT // UNIT
OUT_UNITS = 2
FFN_UNITS = FTILES * (IN_UNITS + OUT_UNITS)
B_TILES = 2
CV_TILES = 4
CONV_TILES = B_TILES + CV_TILES
CONV_UNITS = CONV_TILES * IN_UNITS + KC
POOL_UNITS = 2
POOL_WINDOWS = (2, 4, 8, 16)
HEADS = 16
KV_HEADS = 2
HD = 64
QKV = (HEADS + 2 * KV_HEADS) * HD
NQK = HEADS + KV_HEADS
KV_UNITS = 2
ITEMS = 6
GROUP = 8
ATTN_UNITS = 2 * IN_UNITS + KV_UNITS + KC
BAND = 384
EPS = 1e-6
TAPS = 3

FFN, CONV, POOL, ATTN = "ffn", "conv", "pool", "attn"
UNITS = {FFN: FFN_UNITS, CONV: CONV_UNITS, POOL: POOL_UNITS, ATTN: ATTN_UNITS}
TILE, SCORES, VALUES, ITEM, PROBS, OUTPUT = "tile", "scores", "values", "item", "probs", "output"
ATTN_INS = ([(TILE, 0, 0), (TILE, 0, 1), (TILE, 1, 0), (TILE, 1, 1), (TILE, 2, 0)]
            + [(SCORES, 0, t) for t in range(2) for _ in range(4)]
            + [(TILE, 2, 1), (VALUES, 0, 0), (VALUES, 0, 1)]
            + [(SCORES, 1, t) for t in range(2) for _ in range(4)]
            + [(VALUES, 1, 0), (VALUES, 1, 1)])
ATTN_TURNS = ([(ITEM, i) for i in range(5)] + [(PROBS, 0, 0)] * 2 + [(PROBS, 0, 1)] * 4
              + [(ITEM, 5), (OUTPUT, 0, 0), (OUTPUT, 0, 1)]
              + [(PROBS, 1, 0)] * 2 + [(PROBS, 1, 1)] * 4 + [(OUTPUT, 1, 0), (OUTPUT, 1, 1)])


def in_at(*what):
    return ATTN_INS.index(what)


def turn_at(*what):
    return ATTN_TURNS.index(what)


def prob_blocks(t):
    return [(head, kb) for head in range(GROUP) for kb in range(t + 1)]


def prob_at(t):
    return t * GROUP


INS = {FFN: 2 * FTILES, CONV: 2 * CONV_TILES, POOL: 0, ATTN: len(ATTN_INS)}
FILLS = {FFN: 2 * FTILES, CONV: 2 * CONV_TILES, POOL: 0, ATTN: len(ATTN_TURNS)}
ACCS = 2
NORM_FILLS = 4


class Phase:

    def __init__(self, kind, index, layer, before):
        self.kind, self.index, self.layer = kind, index, layer
        self.nth = layer // 3 if kind == CONV else 0
        self.unit = before.unit + UNITS[before.kind] if before else 0
        self.into = before.into + INS[before.kind] if before else 0
        self.norm_fill = before.fill + FILLS[before.kind] if before else 0
        self.fill = self.norm_fill + NORM_FILLS
        self.acc = before.acc + ACCS if before else 0
        self.next_unit = self.unit + UNITS[kind]


def make_phases():
    phases = []
    for layer, mixer in enumerate((CONV, POOL, ATTN, CONV)):
        for kind in (FFN, mixer, FFN):
            phases.append(Phase(kind, len(phases), layer, phases[-1] if phases else None))
    return phases


def build(nc, stream, x_in, gains, taps, pool_b, pool_scale, b_qkv, q_gain, k_gain, sinks, b_o,
          rel_bias, ident_in, band_in, onehot_in, mask_in, table, spread, out):
    phases = make_phases()
    units_total = phases[-1].next_unit
    assert units_total % RING == 0 and all(p.into % 2 == 0 and p.fill % 2 == 0 for p in phases)

    ctx = ExitStack()
    with ctx:
        def sb(name, shape, dt=F32):
            return ctx.enter_context(nc.sbuf_tensor(name, shape, dt))

        def sem(name):
            return ctx.enter_context(nc.semaphore(name))

        raw = sb("raw", [P, RING, UNIT])
        w_hi = sb("w_hi", [P, RING, UNIT], F32R)
        w_lo = sb("w_lo", [P, RING, UNIT], F32R)
        x = sb("x", [P, HALVES, D])
        xn = sb("xn", [P, HALVES, D])
        h_hi = sb("h_hi", [P, HALVES, KC, P], F32R)
        h_lo = sb("h_lo", [P, HALVES, KC, P], F32R)
        u_hi = sb("u_hi", [P, HALVES, KC, P], F32R)
        u_lo = sb("u_lo", [P, HALVES, KC, P], F32R)
        gain = sb("gain", [P, 2, D])
        squares = sb("squares", [P, HALVES, D], mybir.dt.bfloat16)
        meansq = sb("meansq", [P, HALVES])
        padded = sb("padded", [P, HALVES])
        rstd = sb("rstd", [P, HALVES])
        neg_half = sb("neg_half", [P, GROUP])
        gated = sb("gated", [P, HALVES, FT])
        act = sb("act", [P, HALVES, FT])
        ident = sb("ident", [P, P])
        MIX = 15616
        mix = sb("mix", [P, MIX])
        tap = sb("tap", [P, 2, TAPS, KC])

        def part(at, *shape):
            n = 1
            for s in shape:
                n *= s
            assert at + n <= MIX
            names = " ".join("abc"[:len(shape)])
            kw = {c: s for c, s in zip("abc", shape)}
            return mix[:, at:at + n].rearrange(f"p ({names}) -> p {names}", **kw), at + n

        z_t, a = part(0, KC, SEQ + TAPS - 1)
        b_t, a = part(a, KC, SEQ)
        b_rows, a = part(a, HALVES, 512)
        product, a = part(a, 2, SEQ)
        averaging, a = part(0, 4, 2, SEQ)
        pool_rows, a = part(a, 2, D)
        pool_y, a = part(a, HALVES, D)
        rel_space, a = part(a, 3 * BAND + HEADS)
        onehot = rel_space[0:32, 0:BAND]
        rel_in = rel_space[0:32, 3 * BAND:3 * BAND + HEADS]
        mask_rows = rel_space[0:HEADS, BAND:2 * BAND]
        rel_rows = rel_space[0:HEADS, 2 * BAND:3 * BAND]
        rel, a = part(0, HEADS, SEQ)
        scores_1, a = part(a, GROUP, SEQ)
        bias_qkv, _ = part(a + GROUP * P, 1, QKV)
        probs_t, a = part(a, 3 * GROUP, P)
        q_t, a = part(a, HALVES, KC, P)
        qkv, a = part(a, HALVES, QKV)
        k_twice, a = part(a, KV_HEADS, P)
        k_t, a = part(a, KV_HEADS, SEQ)
        qk_sq, a = part(a, 2, 512)
        late = sb("late", [P, GROUP, P])
        b_o_row = late.rearrange("p c k -> p (c k)")
        scores = [late, scores_1]
        qk_gain = sb("qk_gain", [P, 2, HD])
        qk_sum = sb("qk_sum", [P, ITEMS, GROUP])
        qk_mean = sb("qk_mean", [P, ITEMS, GROUP])
        qk_rstd = sb("qk_rstd", [P, ITEMS, GROUP])
        sink_row = sb("sink_row", [P, HEADS])
        soft = sb("soft", [P, HALVES, 7, HEADS])
        MAX, NEG_MAX, SINK, SINK_EXP, SUM, DENOM, RECIP = range(7)

        into = [ctx.enter_context(nc.psum_tensor(f"into{i}", [P, 512], F32)) for i in range(2)]
        turn = [ctx.enter_context(nc.psum_tensor(f"turn{i}", [P, 512], F32)) for i in range(2)]
        accum = [ctx.enter_context(nc.psum_tensor(f"accum{i}", [P, D], F32)) for i in range(2)]

        raw_landed = [sem(f"raw_landed{s}") for s in range(RING)]
        hi_made = sem("hi_made")
        lo_made = sem("lo_made")
        unit_used = sem("unit_used")
        in_done = sem("in_done")
        gate_done = sem("gate_done")
        in_read = sem("in_read")
        turned = sem("turned")
        turn_hi = sem("turn_hi")
        turn_read = sem("turn_read")
        acc_done = sem("acc_done")
        acc_read = sem("acc_read")
        scaled = sem("scaled")
        meansq_done = sem("meansq_done")
        eps_added = sem("eps_added")
        rstd_done = sem("rstd_done")
        vec_step = sem("vec_step")
        x_loaded = [[sem(f"x_loaded{t}_{q}") for q in range(2)] for t in range(HALVES)]
        ident_loaded = sem("ident_loaded")
        taps_loaded = sem("taps_loaded")
        gain_loaded = [sem(f"gain_loaded{i}") for i in range(2)]
        averaging_scaled = sem("averaging_scaled")
        pool_half_done = sem("pool_half_done")
        gain_loaded_first = [sem(f"gain_loaded_first{q}") for q in range(2)]
        pool_loaded = sem("pool_loaded")
        attn_loaded = sem("attn_loaded")
        rel_loaded = sem("rel_loaded")
        rel_turned = sem("rel_turned")
        rel_masked = sem("rel_masked")
        rel_stored = sem("rel_stored")
        rel_spread = sem("rel_spread")
        constants = sem("constants")
        first_tap = sem("first_tap")
        product_done = sem("product_done")
        product_hi = sem("product_hi")
        product_split = sem("product_split")
        bias_added = sem("bias_added")
        squared = sem("squared")
        qk_mean_done = sem("qk_mean_done")
        qk_rstd_done = sem("qk_rstd_done")
        k_ready = sem("k_ready")
        max_done = sem("max_done")
        sink_done = sem("sink_done")
        exp_done = sem("exp_done")
        stored = sem("stored")

        def bank(b, chunks):
            return turn[b][:, 0:chunks * P].rearrange("p (c k) -> p c k", c=chunks)

        block = ctx.enter_context(nc.Block())

        @block.sync
        def _(sp):
            def load_unit(n, s, wait):
                if wait is not None:
                    sp.wait_ge(lo_made, wait)
                sp.dma_start(raw[:, s, :], stream[n]).then_inc(raw_landed[s], 16)

            def load_x(t, q):
                cols = slice(q * 512, (q + 1) * 512)
                sp.dma_start(x[:, t, cols], x_in[t * P:(t + 1) * P, cols]).then_inc(x_loaded[t][q], 16)

            load_x(0, 0)
            load_x(0, 1)
            sp.dma_start(gain[:, 0, 512:D], gains[0, 512:D].partition_broadcast(P)
                         ).then_inc(gain_loaded_first[1], 16)
            load_unit(0, 0, None)
            load_unit(1, 1, None)
            load_x(1, 0)
            load_x(1, 1)
            for s in range(2, RING):
                load_unit(s, s, None)
            with sp.Fori(1, units_total // RING) as i:
                for s in range(RING):
                    load_unit(i * RING + s, s, i * RING + (s + 1 - RING))
            sp.wait_ge(stored, 16 * 2 * HALVES)

        @block.gpsimd
        def _(pool):
            def row(ap):
                return ap.partition_broadcast(P)

            def power(to, of, at):
                return pool.tensor_tensor(to, of, neg_half[:, 0:at], ALU.pow)

            pool.memset(neg_half[:, :], -0.5).then_inc(constants, 1)
            pool.wait_ge(x_loaded[1][1], 16)
            pool.dma_start(tap[:, :, :, :], taps).then_inc(taps_loaded, 16)
            pool.dma_start(gain[:, 1, :], row(gains[1])).then_inc(gain_loaded[1], 16)
            pool.dma_start(qk_gain[:, 0, :], row(q_gain)).then_inc(attn_loaded, 16)
            pool.dma_start(qk_gain[:, 1, :], row(k_gain)).then_inc(attn_loaded, 16)
            pool.dma_start(sink_row[:, :], row(sinks)).then_inc(attn_loaded, 16)
            pool.dma_start(b_o_row, row(b_o)).then_inc(attn_loaded, 16)
            pool.wait_ge(constants, 1)
            for ph in phases:
                for t in range(HALVES):
                    n = 2 * ph.index + t + 1
                    pool.wait_ge(meansq_done, n)
                    pool.tensor_scalar(padded[:, t:t + 1], meansq[:, t:t + 1], 1.0, EPS, ALU.mult,
                                       ALU.add).then_inc(eps_added, 1)
                    pool.wait_ge(eps_added, n)
                    power(rstd[:, t:t + 1], padded[:, t:t + 1], 1).then_inc(rstd_done, 1)
                if ph.index and ph.index + 1 < len(phases):
                    i = (ph.index + 1) % 2
                    pool.wait_ge(scaled, 4 * ph.index)
                    pool.dma_start(gain[:, i, :], row(gains[ph.index + 1])).then_inc(gain_loaded[i], 16)
                if ph.index and phases[ph.index - 1].kind == CONV and ph.layer == 0:
                    pool.wait_ge(product_split, CV_TILES)
                    pool.dma_start(averaging, band_in).then_inc(pool_loaded, 16)
                    pool.dma_start(pool_rows[:, 0, :], row(pool_b)).then_inc(pool_loaded, 16)
                    pool.dma_start(pool_rows[:, 1, :], row(pool_scale)).then_inc(pool_loaded, 16)
                    pool.dma_start(onehot, onehot_in).then_inc(rel_loaded, 16)
                    pool.dma_start(rel_in, rel_bias).then_inc(rel_loaded, 16)
                    pool.dma_start(mask_rows, mask_in).then_inc(rel_loaded, 16)
                if ph.index and phases[ph.index - 1].kind == POOL:
                    pool.wait_ge(rel_masked, 1)
                    pool.dma_start(table, rel_rows).then_inc(rel_stored, 16)
                    pool.wait_ge(rel_stored, 16)
                    pool.dma_start(spread.rearrange("q (h k) -> h q k", h=HEADS),
                                   bass.AP(table.tensor, P - 1, [[BAND, HEADS], [-1, P], [1, SEQ]])
                                   ).then_inc(rel_stored, 16)
                    pool.wait_ge(rel_stored, 32)
                    pool.wait_ge(acc_read, 2 * ph.acc)
                    pool.dma_start(rel.rearrange("p h k -> p (h k)"), spread).then_inc(rel_spread, 16)
                    pool.dma_start(bias_qkv[:, 0, :], row(b_qkv)).then_inc(attn_loaded, 16)
                if ph.kind == ATTN:
                    for i in range(ITEMS):
                        n = GROUP if i >= 2 else KV_HEADS
                        if i == 2:
                            pool.wait_ge(scaled, 4 * ph.index + 4)
                            for t in range(HALVES):
                                pool.tensor_tensor(x[:, t, :], x[:, t, :], b_o_row,
                                                   ALU.add).then_inc(bias_added, 1)
                        pool.wait_ge(qk_mean_done, i + 1)
                        power(qk_rstd[:, i, 0:n], qk_mean[:, i, 0:n], n).then_inc(qk_rstd_done, 1)

        @block.tensor
        def _(pe):
            def release_here(ins, yes):
                if yes:
                    ins.then_inc(unit_used, 1)

            def in_half(ph, i, t, unit, slots, cols=512, units=IN_UNITS, release=False, first_tile=False,
                        fill=None, between=None):
                h = ph.into + i * 2 + t if fill is None else fill
                if not (isinstance(h, int) and h < 2):
                    pe.wait_ge(in_read, h - 1)
                per = KC // units
                for u in range(units):
                    s = slots[u]
                    for k in range(per):
                        c = u * per + k
                        if t == 0 and k == 0:
                            pe.wait_ge(hi_made, unit + (u + 1))
                        if first_tile and c % 4 == 0:
                            pe.wait_ge(turn_read, ph.norm_fill + 2 * t + c // 4 + 1)
                        wh = w_hi[:, s, k * cols:(k + 1) * cols]
                        wl = w_lo[:, s, k * cols:(k + 1) * cols]
                        o = into[t][:, 0:cols]
                        m = pe.matmul(o, h_hi[:, t, c, :], wh, start=(c == 0), stop=False)
                        release_here(m, release and c == 0)
                        pe.matmul(o, h_lo[:, t, c, :], wh, start=False, stop=False)
                        if t == 0 and k == 0:
                            pe.wait_ge(lo_made, unit + (u + 1))
                        last = pe.matmul(o, h_hi[:, t, c, :], wl, start=False, stop=(c == KC - 1))
                        if between:
                            between(c)
                    if t == 1 and u < units - 1:
                        last.then_inc(unit_used, 1)
                last.then_inc(in_done, 1)

            def turn_half(fill, b, source, chunks, ready, release=False):
                if ready is not None:
                    pe.wait_ge(*ready)
                if not (isinstance(fill, int) and fill < 2):
                    pe.wait_ge(turn_read, fill - 1)
                for c in range(chunks):
                    last = pe.transpose(turn[b][:, c * P:(c + 1) * P], source[:, c * P:(c + 1) * P],
                                        ident[:, :])
                    release_here(last, release and c == 0)
                last.then_inc(turned, 1)

            def norm_turn(ph, t, q):
                turn_half(ph.norm_fill + 2 * t + q, q, xn[:, t, q * 512:(q + 1) * 512], 4,
                          (scaled, 4 * ph.index + 2 * t + q + 1))

            def half_1_turns(ph, first, second):
                def after(c):
                    if c in (first, second):
                        norm_turn(ph, 1, (first, second).index(c))
                return after

            def norm_turns(ph, t):
                if ph is not None and ph.kind != POOL:
                    for q in range(2):
                        norm_turn(ph, t, q)

            def out_unit(t, unit, s, k, start, stop, release=False):
                if t == 0:
                    pe.wait_ge(lo_made, unit + 1)
                for n, (stat, w) in enumerate(((u_hi, w_hi), (u_lo, w_hi), (u_hi, w_lo))):
                    for half in range(2):
                        cols = slice(half * 512, half * 512 + 512)
                        last = pe.matmul(accum[t][:, cols], stat[:, t, k, :], w[:, s, cols],
                                         start=(start and n == 0), stop=(stop and n == 2))
                        release_here(last, release and n == 0 and half == 0)
                return last

            def acc_free(acc):
                if acc >= 2:
                    pe.wait_ge(acc_read, 2 * (acc - 1))

            def out_block(ph, t, unit, k0, k1, ready, release=False):
                if k0 == 0:
                    acc_free(ph.acc + t)
                for k in range(k0, k1):
                    ready(t, k)
                    n = unit + k
                    last = out_unit(t, n, n % RING, k, k == 0, k == KC - 1, release and k == k0)
                    if k == KC - 1:
                        last.then_inc(acc_done, 1)
                    elif t == 1:
                        last.then_inc(unit_used, 1)

            def ffn(ph, nxt):
                def in_tile(j, t, first=False, release=False):
                    unit = ph.unit if first else ph.unit + IN_UNITS + (j - 1) * RING
                    at = 0 if first else IN_UNITS
                    in_half(ph, j, t, unit, [(ph.unit + at + u) % RING for u in range(IN_UNITS)],
                            release=release, first_tile=first,
                            between=half_1_turns(ph, 3, 5) if first and t == 0 else None)

                def turns(j, t, release=False):
                    turn_half(ph.fill + (j * 2 + t), t, act[:, t, :], 2,
                              (in_read, ph.into + (j * 2 + (t + 1))), release)

                def down(j, t, first=False, last=False, release=False, ks=range(OUT_UNITS)):
                    at = 2 * IN_UNITS if not last else FFN_UNITS - OUT_UNITS
                    unit = ph.unit + 2 * IN_UNITS + j * RING if not last else ph.unit + at
                    if first:
                        acc_free(ph.acc + t)
                    pe.wait_ge(turn_read, ph.fill + (j * 2 + (t + 1)))
                    for k in ks:
                        end = last and k == OUT_UNITS - 1
                        m = out_unit(t, unit + k, (ph.unit + at + k) % RING, k + (2 if last else 0),
                                     first and k == 0, end, release and k == 0)
                        if end:
                            m.then_inc(acc_done, 1)
                        elif t == 1:
                            m.then_inc(unit_used, 1)

                def tile(j, first=False):
                    in_tile(j, 0, release=first)
                    turns(j - 1, 0)
                    turns(j - 1, 1)
                    in_tile(j, 1)
                    down(j - 1, 0, first=first, release=True)
                    down(j - 1, 1, first=first)

                end = FTILES - 1
                in_tile(0, 0, first=True, release=ph.index > 0)
                in_tile(0, 1, first=True)
                tile(1, first=True)
                with pe.Fori(2, end) as j:
                    tile(j)
                in_tile(end, 0)
                turns(end - 1, 0)
                turns(end - 1, 1)
                in_tile(end, 1)
                turns(end, 0, release=True)
                down(end - 1, 0)
                turns(end, 1)
                down(end, 0, last=True)
                down(end - 1, 1)
                down(end, 1, last=True, ks=(0,))
                norm_turns(nxt, 0)
                down(end, 1, last=True, ks=(1,))

            def conv_mixer(ph, nxt):
                def turns(i, t):
                    rows_of = b_rows if i < B_TILES else act
                    turn_half(ph.fill + 2 * i + t, t, rows_of[:, t, :], 4 if i < B_TILES else 2,
                              (in_read, ph.into + 2 * i + t + 1), t == 0 and i < CONV_TILES - 1)

                for i in range(CONV_TILES):
                    unit = ph.unit + IN_UNITS * i
                    slots = [(unit + u) % RING for u in range(IN_UNITS)]
                    in_half(ph, i, 0, unit, slots, release=(i == 0), first_tile=(i == 0),
                            between=half_1_turns(ph, 3, 5) if i == 0 else None)
                    if i:
                        turns(i - 1, 1)
                    in_half(ph, i, 1, unit, slots, first_tile=(i == 0))
                    turns(i, 0)
                base = CV_TILES * ph.nth

                def ready(t, k):
                    if k % 2 == 0:
                        pe.wait_ge(product_split, base + k // 2 + 1)

                unit = ph.unit + CONV_TILES * IN_UNITS
                out_block(ph, 0, unit, 0, 2, ready, release=True)
                turns(CONV_TILES - 1, 1)
                out_block(ph, 0, unit, 2, 4, ready)
                out_block(ph, 1, unit, 0, 4, ready)
                out_block(ph, 0, unit, 4, KC, ready)
                out_block(ph, 1, unit, 4, KC - 1, ready)
                norm_turns(nxt, 0)
                out_block(ph, 1, unit, KC - 1, KC, ready)

            def pool_mixer(ph, nxt):
                pe.wait_ge(rel_loaded, 48)
                pe.wait_ge(in_read, ph.into)
                pe.matmul(into[0][0:HEADS, 0:BAND], rel_in, onehot, start=True,
                          stop=True).then_inc(rel_turned, 1)
                pe.wait_ge(averaging_scaled, HALVES)
                pe.wait_ge(scaled, 4 * ph.index + 4)
                for q in range(4):
                    pe.wait_ge(turn_read, ph.norm_fill + q - 1)
                    for k in range(2):
                        c = 2 * q + k
                        cols = slice(c * P, (c + 1) * P)
                        m = pe.matmul(turn[q % 2][:, k * SEQ:(k + 1) * SEQ], xn[:, 0, cols],
                                      averaging[:, q, 0, :], start=True, stop=False)
                        release_here(m, c == 0)
                        last = pe.matmul(turn[q % 2][:, k * SEQ + P:(k + 1) * SEQ], xn[:, 1, cols],
                                         averaging[:, q, 1, P:SEQ], start=False, stop=True)
                    last.then_inc(turned, 1)
                for t in range(HALVES):
                    acc_free(ph.acc + t)
                    for g in range(4):
                        if t == 0:
                            pe.wait_ge(turn_read, ph.norm_fill + g + 1)
                            pe.wait_ge(lo_made, ph.unit + g // 2 + 1)
                        s = (ph.unit + g // 2) % RING
                        o = accum[t][:, g * FT:(g + 1) * FT]
                        for k in range(2):
                            c = 2 * g + k
                            cols = slice(((g % 2) * 2 + k) * FT, ((g % 2) * 2 + k + 1) * FT)
                            first = pe.matmul(o, h_hi[:, t, c, :], w_hi[:, s, cols], start=(k == 0),
                                              stop=False)
                            if c == KC // 2:
                                first.then_inc(pool_half_done, 1)
                            pe.matmul(o, h_lo[:, t, c, :], w_hi[:, s, cols], start=False, stop=False)
                            last = pe.matmul(o, h_hi[:, t, c, :], w_lo[:, s, cols], start=False,
                                             stop=(k == 1))
                        if t == 1 and g == 1:
                            last.then_inc(unit_used, 1)
                    last.then_inc(acc_done, 1)
                norm_turns(nxt, 0)
                pe.wait_ge(rel_masked, 1)

            def attn_mixer(ph, nxt):
                def item_turn(i, release=False):
                    t = i % 2
                    if i < 2:
                        source, chunks, ready = k_twice.rearrange("p a b -> p (a b)"), 2, (k_ready, i + 1)
                    else:
                        source, chunks = qkv[:, t, (i // 2 - 1) * 512:(i // 2) * 512], 4
                        ready = (in_read, ph.into + in_at(TILE, i // 2, t) + 1)
                    f = ph.fill + turn_at(ITEM, i)
                    turn_half(f, f % 2, source, chunks, ready, release)

                def score_fills(g, t):
                    keys = (t + 1) * P
                    pe.wait_ge(turn_read, ph.fill + turn_at(ITEM, 2 + 2 * g + t) + 1)
                    for b in range(GROUP // 2):
                        h = ph.into + in_at(SCORES, g, t) + b
                        pe.wait_ge(in_read, h - 1)
                        odd = b % 2
                        for m in range(2):
                            head = g * GROUP + 4 * (b // 2) + 2 * m + odd
                            last = pe.matmul(into[h % 2][:, m * SEQ:m * SEQ + keys],
                                             q_t[odd * HD:(odd + 1) * HD, t, head // 2, :],
                                             k_t[odd * HD:(odd + 1) * HD, head // 8, 0:keys],
                                             start=True, stop=True)
                        last.then_inc(in_done, 1)

                def prob_turns(g, t, n0, n1):
                    for n in range(n0, n1):
                        four = prob_blocks(t)[4 * n:4 * n + 4]
                        pe.wait_ge(exp_done, (2 * g + t) * GROUP + four[-1][0] + 1)
                        f = ph.fill + turn_at(PROBS, g, t) + n
                        pe.wait_ge(turn_read, f - 1)
                        for m, (head, kb) in enumerate(four):
                            last = pe.transpose(turn[f % 2][:, m * P:(m + 1) * P],
                                                scores[t][:, head, kb * P:(kb + 1) * P], ident[:, :])
                        last.then_inc(turned, 1)

                def values(g, t, release=False):
                    h = ph.into + in_at(VALUES, g, t)
                    pe.wait_ge(turn_read, ph.fill + turn_at(PROBS, g, t) + 2 * (t + 1))
                    pe.wait_ge(in_read, h - 1)
                    at = NQK * HD + g * HD
                    for n, (head, kb) in enumerate(prob_blocks(t)):
                        last = pe.matmul(into[h % 2][:, head * HD:(head + 1) * HD],
                                         probs_t[:, prob_at(t) + n, :], qkv[:, kb, at:at + HD],
                                         start=(kb == 0), stop=(kb == t))
                        release_here(last, release and n == 0)
                    last.then_inc(in_done, 1)

                def output_turn(g, t):
                    f = ph.fill + turn_at(OUTPUT, g, t)
                    turn_half(f, f % 2, xn[:, t, g * 512:(g + 1) * 512], 4,
                              (in_read, ph.into + in_at(VALUES, g, t) + 1))

                def ready(t, k):
                    if k % 4 == 0:
                        pe.wait_ge(turn_read, ph.fill + turn_at(OUTPUT, k // 4, t) + 1)

                def tile(i, t, release=False, between=None):
                    unit, units, cols = ((ph.unit, KV_UNITS, 256), (ph.unit + KV_UNITS, IN_UNITS, 512),
                                         (ph.unit + KV_UNITS + IN_UNITS, IN_UNITS, 512))[i]
                    in_half(ph, i, t, unit, [(unit + u) % RING for u in range(units)], cols, units,
                            release=release, first_tile=(i == 0), fill=ph.into + in_at(TILE, i, t),
                            between=between)

                tile(0, 0, release=True, between=half_1_turns(ph, 5, 7))
                tile(0, 1)
                tile(1, 0, release=True)
                item_turn(0)
                tile(1, 1)
                item_turn(1, release=True)
                item_turn(2)
                tile(2, 0)
                item_turn(3)
                score_fills(0, 0)
                score_fills(0, 1)
                item_turn(4)
                tile(2, 1, between=lambda c: prob_turns(0, 0, 0, 2) if c == 6 else None)
                values(0, 0, release=True)
                prob_turns(0, 1, 0, 4)
                item_turn(5)
                output_turn(0, 0)
                values(0, 1)
                score_fills(1, 0)
                output_turn(0, 1)
                score_fills(1, 1)
                unit = ph.unit + KV_UNITS + 2 * IN_UNITS
                out_block(ph, 0, unit, 0, 4, ready)
                prob_turns(1, 0, 0, 2)
                out_block(ph, 1, unit, 0, 1, ready)
                values(1, 0)
                prob_turns(1, 1, 0, 2)
                out_block(ph, 1, unit, 1, 2, ready)
                prob_turns(1, 1, 2, 4)
                out_block(ph, 1, unit, 2, 3, ready)
                values(1, 1)
                output_turn(1, 0)
                out_block(ph, 1, unit, 3, 4, ready)
                output_turn(1, 1)
                out_block(ph, 0, unit, 4, KC, ready)
                out_block(ph, 1, unit, 4, KC - 1, ready)
                norm_turns(nxt, 0)
                out_block(ph, 1, unit, KC - 1, KC, ready)

            pe.wait_ge(ident_loaded, 16)
            norm_turns(phases[0], 0)
            for ph, nxt in zip(phases, phases[1:] + [None]):
                {FFN: ffn, CONV: conv_mixer, POOL: pool_mixer, ATTN: attn_mixer}[ph.kind](ph, nxt)

        @block.scalar
        def _(sc):
            def hi_unit(s, landed, wait):
                sc.wait_ge(raw_landed[s], landed)
                if wait is not None:
                    sc.wait_ge(unit_used, wait)
                sc.activation(w_hi[:, s, :], raw[:, s, :], ACT.Copy).then_inc(hi_made, 1)

            def hi_units(n0, n1):
                for n in range(n0, n1):
                    hi_unit(n % RING, 16 * (n // RING + 1), n - RING + 1 if n >= RING else None)

            def turn_split(b, to, f):
                sc.wait_ge(turned, f)
                sc.activation(to, bank(b, to.shape[1]), ACT.Copy).then_inc(turn_hi, 1)

            def mean_square(ph, t):
                if ph.index:
                    sc.wait_ge(acc_read, 2 * (ph.acc - 1 + t))
                else:
                    for q in range(2):
                        sc.wait_ge(x_loaded[t][q], 16)
                sc.activation(squares[:, t, :], x[:, t, :], ACT.Square, scale=D ** -0.5,
                              accum_out=meansq[:, t:t + 1]).then_inc(meansq_done, 1)

            def next_units(ph):
                hi_units(max(ph.next_unit, ph.unit + IN_UNITS), min(ph.next_unit + IN_UNITS, units_total))

            def boundary(ph):
                for t in range(HALVES):
                    if ph.index or t:
                        mean_square(ph, t)
                    if ph.kind == POOL:
                        if t == 0:
                            sc.wait_ge(pool_loaded, 48)
                        sc.wait_ge(rstd_done, 2 * ph.index + t + 1)
                        part_of = averaging[:, :, t, t * P:SEQ]
                        sc.activation(part_of, part_of, ACT.Copy,
                                      scale=rstd[:, t:t + 1]).then_inc(averaging_scaled, 1)
                    else:
                        for q in range(2):
                            turn_split(q, h_hi[:, t, 4 * q:4 * q + 4, :], ph.norm_fill + 2 * t + q + 1)
                    if ph.index == 0 and t == 0:
                        hi_units(0, 2)
                        mean_square(ph, t)
                        hi_units(2, IN_UNITS)
                sc.wait_ge(rstd_done, 2 * ph.index + 2)

            def gate(ph, i, t, func):
                sc.wait_ge(in_done, ph.into + (i * 2 + (t + 1)))
                sc.activation(gated[:, t, :], into[t][:, 0:FT], func,
                              scale=rstd[:, t:t + 1]).then_inc(gate_done, 1)

            def ffn(ph):
                def ahead(j, a, b):
                    for u in range(a, b):
                        at = ph.unit + IN_UNITS + u
                        if isinstance(j, int):
                            hi_units(at + RING * j, at + RING * j + 1)
                        else:
                            hi_unit(at % RING, (j + (at // RING + 1)) * 16, j * RING + (at - RING + 1))

                def split(j, t, k=0):
                    turn_split(t, u_hi[:, t, k:k + 2, :], ph.fill + (j * 2 + (t + 1)))

                def tile(j, first=False):
                    gate(ph, j, 0, ACT.Silu)
                    if not first:
                        split(j - 1, 0)
                        split(j - 1, 1)
                    ahead(j, 0, IN_UNITS)
                    gate(ph, j, 1, ACT.Silu)
                    ahead(j, IN_UNITS, RING)

                end = FTILES - 1
                tile(0, first=True)
                with sc.Fori(1, end) as j:
                    tile(j)
                gate(ph, end, 0, ACT.Silu)
                split(end - 1, 0)
                split(end - 1, 1)
                gate(ph, end, 1, ACT.Silu)
                split(end, 0, 2)
                hi_units(ph.next_unit - OUT_UNITS, ph.next_unit)
                split(end, 1, 2)

            def conv_mixer(ph):
                out0 = ph.unit + CONV_TILES * IN_UNITS

                def product_split_hi(m):
                    sc.wait_ge(product_done, CV_TILES * ph.nth + m + 1)
                    sc.activation(u_hi[:, :, 2 * m:2 * m + 2, :].rearrange("p t c k -> p c t k"),
                                  product.rearrange("p c (t k) -> p c t k", t=HALVES),
                                  ACT.Copy).then_inc(product_hi, 1)

                def tap_one(m):
                    sc.wait_ge(turn_read, ph.fill + 2 * (m + B_TILES) + 2)
                    if m or ph.nth:
                        sc.wait_ge(product_split, CV_TILES * ph.nth + m)
                    for c in range(2):
                        n = 2 * m + c
                        ins = sc.activation(product[:, c, :], z_t[:, n, 0:SEQ], ACT.Copy,
                                            scale=tap[:, ph.nth, 0, n:n + 1])
                    ins.then_inc(first_tap, 1)

                sc.wait_ge(taps_loaded, 16)
                for i in range(CONV_TILES):
                    nxt = ph.unit + IN_UNITS * (i + 1)
                    if i >= B_TILES:
                        gate(ph, i, 0, ACT.Copy)
                    hi_units(nxt, nxt + 2)
                    if i > B_TILES:
                        tap_one(i - 1 - B_TILES)
                    hi_units(nxt + 2, nxt + IN_UNITS)
                    if i >= B_TILES:
                        gate(ph, i, 1, ACT.Copy)
                    if i > B_TILES:
                        product_split_hi(i - 1 - B_TILES)
                tap_one(CV_TILES - 1)
                hi_units(out0 + 4, out0 + 6)
                product_split_hi(CV_TILES - 1)
                hi_units(out0 + 6, out0 + KC)

            def pool_mixer(ph):
                for q in range(4):
                    sc.wait_ge(turned, ph.norm_fill + q + 1)
                    sc.activation(h_hi[:, :, 2 * q:2 * q + 2, :].rearrange("p t c k -> p c t k"),
                                  turn[q % 2][:, :].rearrange("p (c t k) -> p c t k", c=2, t=2),
                                  ACT.Copy).then_inc(turn_hi, 1)

            def attn_mixer(ph):
                q0 = ph.unit + KV_UNITS
                out0 = q0 + 2 * IN_UNITS

                def square(i):
                    t = i % 2
                    cols = slice(D, D + P) if i < 2 else slice((i // 2 - 1) * 512, (i // 2) * 512)
                    n = P if i < 2 else 512
                    sc.wait_ge(in_read, ph.into + in_at(TILE, i // 2, t) + 1)
                    if i >= 2:
                        sc.wait_ge(qk_mean_done, i - 1)
                    sc.activation(qk_sq[:, i % 2, 0:n], qkv[:, t, cols], ACT.Square,
                                  scale=HD ** -0.5).then_inc(squared, 1)

                def exps(g, t):
                    heads = slice(g * GROUP, (g + 1) * GROUP)
                    sc.wait_ge(max_done, 2 * g + t + 1)
                    sc.activation(soft[:, t, SINK_EXP, heads], soft[:, t, SINK, heads],
                                  ACT.Exp).then_inc(sink_done, 1)
                    for head in range(GROUP):
                        keys = scores[t][:, head, 0:(t + 1) * P]
                        n = g * GROUP + head
                        sc.activation(keys, keys, ACT.Exp, bias=soft[:, t, NEG_MAX, n:n + 1],
                                      accum_out=soft[:, t, SUM, n:n + 1]).then_inc(exp_done, 1)

                def output_split(g, t):
                    f = ph.fill + turn_at(OUTPUT, g, t)
                    turn_split(f % 2, u_hi[:, t, 4 * g:4 * g + 4, :], f + 1)

                square(0)
                hi_units(q0 + 2, q0 + 4)
                square(1)
                hi_units(q0 + 4, q0 + 6)
                square(2)
                hi_units(q0 + 6, q0 + 8)
                square(3)
                hi_units(out0, out0 + 2)
                square(4)
                exps(0, 0)
                exps(0, 1)
                square(5)
                hi_units(out0 + 2, out0 + 6)
                output_split(0, 0)
                output_split(0, 1)
                exps(1, 0)
                exps(1, 1)
                hi_units(out0 + 6, out0 + KC)
                output_split(1, 0)
                output_split(1, 1)

            sc.dma_start(gain[:, 0, 0:512], gains[0, 0:512].partition_broadcast(P)
                         ).then_inc(gain_loaded_first[0], 16)
            sc.dma_start(ident[:, :], ident_in).then_inc(ident_loaded, 16)
            for ph in phases:
                boundary(ph)
                {FFN: ffn, CONV: conv_mixer, POOL: pool_mixer, ATTN: attn_mixer}[ph.kind](ph)
                next_units(ph)
            acc = phases[-1].acc
            for t in range(HALVES):
                for q in range(2):
                    cols = slice(q * 512, (q + 1) * 512)
                    sc.wait_ge(acc_read, 2 * (acc + t) + q + 1)
                    sc.dma_start(out[t * P:(t + 1) * P, cols], x[:, t, cols]).then_inc(stored, 16)

        @block.vector
        def _(ve):
            steps = [0]
            turn_his = [0]
            gates = [0]

            def step(ins):
                steps[0] += 1
                ins.then_inc(vec_step, 1)

            def settle():
                ve.wait_ge(vec_step, steps[0])

            def link(ins):
                step(ins)
                settle()

            def lo_unit(s, made):
                ve.wait_ge(hi_made, made)
                ve.tensor_tensor(w_lo[:, s, :], raw[:, s, :], w_hi[:, s, :].bitcast(F32),
                                 ALU.subtract).then_inc(lo_made, 1)

            def lo_units(n0, n1):
                for n in range(n0, n1):
                    lo_unit(n % RING, n + 1)

            def turn_split(b, to, hi, count):
                ve.wait_ge(turn_hi, count)
                ve.tensor_tensor(to, bank(b, to.shape[1]), hi.bitcast(F32),
                                 ALU.subtract).then_inc(turn_read, 1)

            def residual(ph, t, q):
                cols = slice(q * 512, (q + 1) * 512)
                if ph.kind == POOL and q == 0:
                    ve.wait_ge(pool_half_done, t + 1)
                elif ph.kind == POOL or q == 0:
                    ve.wait_ge(acc_done, ph.acc + t + 1)
                if ph.kind == POOL:
                    y = pool_y[:, t, cols]
                    link(ve.tensor_tensor(y, accum[t][:, cols], pool_rows[:, 1, cols], ALU.mult))
                    ins = ve.tensor_tensor(x[:, t, cols], y, x[:, t, cols], ALU.add)
                else:
                    ins = ve.scalar_tensor_tensor(out=x[:, t, cols], in0=accum[t][:, cols],
                                                  scalar=0.5 if ph.kind == FFN else 1.0,
                                                  in1=x[:, t, cols], op0=ALU.mult, op1=ALU.add)
                ins.then_inc(acc_read, 1)

            def boundary(prev, ph):
                def scale(t, q):
                    cols = slice(q * 512, (q + 1) * 512)
                    if prev is not None:
                        ve.wait_ge(acc_read, 2 * (ph.acc - 2 + t) + q + 1)
                    ve.tensor_tensor(xn[:, t, cols], x[:, t, cols], gain[:, ph.index % 2, cols],
                                     ALU.mult).then_inc(scaled, 1)

                def turns_split(t):
                    for q in range(2):
                        turn_his[0] += 1
                        turn_split(q, h_lo[:, t, 4 * q:4 * q + 4, :], h_hi[:, t, 4 * q:4 * q + 4, :],
                                   turn_his[0])

                early = ph.unit + 2
                if prev is not None:
                    lo_units(max(ph.unit, prev.unit + IN_UNITS), early)
                    ve.wait_ge(gain_loaded[ph.index % 2], 16 * ((ph.index + 1) // 2))
                for t in range(HALVES):
                    if ph.kind == POOL:
                        residual(prev, t, 0)
                        residual(prev, t, 1)
                    for q in range(2):
                        if prev is None:
                            ve.wait_ge(gain_loaded_first[q], 16)
                            ve.wait_ge(x_loaded[t][q], 16)
                        elif ph.kind != POOL:
                            residual(prev, t, q)
                        scale(t, q)
                    last_units = (early if prev is None else early + 1, ph.unit + IN_UNITS)
                    if t == 0 and prev is not None:
                        lo_units(early, early + 1)
                    if t == 1 and ph.kind != ATTN:
                        lo_units(*last_units)
                    if ph.kind != POOL:
                        turns_split(t)
                    if t == 0 and prev is None:
                        lo_units(ph.unit, early)
                    if t == 1 and ph.kind == ATTN:
                        lo_units(*last_units)
                ve.wait_ge(rstd_done, 2 * ph.index + 2)

            def times(ph, i, t):
                ve.wait_ge(gate_done, gates[0] + (i * 2 + (t + 1)))
                ve.scalar_tensor_tensor(out=act[:, t, :], in0=into[t][:, FT:2 * FT],
                                        scalar=rstd[:, t:t + 1], in1=gated[:, t, :], op0=ALU.mult, op1=ALU.mult).then_inc(in_read, 1)

            def ffn(ph):
                his = turn_his[0]

                def ahead(j, a, b):
                    for u in range(a, b):
                        at = ph.unit + IN_UNITS + u
                        lo_unit(at % RING, j * RING + (at + 1))

                def split(j, t, k=0):
                    turn_split(t, u_lo[:, t, k:k + 2, :], u_hi[:, t, k:k + 2, :], his + (j * 2 + (t + 1)))

                def product_of(j, t, first=False):
                    if not first:
                        ve.wait_ge(turned, ph.fill + ((j - 1) * 2 + (t + 1)))
                    times(ph, j, t)

                def tile(j, first=False):
                    product_of(j, 0, first)
                    if not first:
                        split(j - 1, 0)
                        split(j - 1, 1)
                    ahead(j, 0, IN_UNITS)
                    product_of(j, 1, first)
                    ahead(j, IN_UNITS, RING)

                end = FTILES - 1
                tile(0, first=True)
                with ve.Fori(1, end) as j:
                    tile(j)
                product_of(end, 0)
                split(end - 1, 0)
                split(end - 1, 1)
                product_of(end, 1)
                split(end, 0, 2)
                lo_units(ph.next_unit - OUT_UNITS, ph.next_unit)
                split(end, 1, 2)
                gates[0] += 2 * FTILES
                turn_his[0] += 2 * FTILES

            def conv_mixer(ph):
                out0 = ph.unit + CONV_TILES * IN_UNITS
                base = CV_TILES * ph.nth

                def b_turned(i, t):
                    ve.wait_ge(turned, ph.fill + 2 * i + t + 1)
                    ve.tensor_copy(b_t[:, 4 * i:4 * i + 4, t * P:(t + 1) * P],
                                   bank(t, 4)).then_inc(turn_read, 1)

                def z_turned(i, t):
                    m = i - B_TILES
                    ve.wait_ge(turned, ph.fill + 2 * i + t + 1)
                    a = TAPS - 1 + t * P
                    ve.tensor_copy(z_t[:, 2 * m:2 * m + 2, a:a + P], bank(t, 2)).then_inc(turn_read, 1)

                def convolve(m):
                    ve.wait_ge(turn_read, ph.fill + 2 * (m + B_TILES) + 2)
                    ve.wait_ge(first_tap, base + m + 1)
                    for tp in range(1, TAPS):
                        for c in range(2):
                            z = z_t[:, 2 * m + c, tp:tp + SEQ]
                            o = product[:, c, :]
                            w = tap[:, ph.nth, tp, 2 * m + c:2 * m + c + 1]
                            step(ve.scalar_tensor_tensor(out=o, in0=z, scalar=w, in1=o,
                                                         op0=ALU.mult, op1=ALU.add))
                        settle()
                    ve.tensor_tensor(product, product, b_t[:, 2 * m:2 * m + 2, :],
                                     ALU.mult).then_inc(product_done, 1)

                def product_lo(m):
                    ve.wait_ge(product_hi, base + m + 1)
                    chunks = slice(2 * m, 2 * m + 2)
                    ve.tensor_tensor(u_lo[:, :, chunks, :].rearrange("p t c k -> p c t k"),
                                     product.rearrange("p c (t k) -> p c t k", t=HALVES),
                                     u_hi[:, :, chunks, :].rearrange("p t c k -> p c t k").bitcast(F32),
                                     ALU.subtract).then_inc(product_split, 1)

                link(ve.memset(z_t[:, :, 0:TAPS - 1], 0.0))
                ve.wait_ge(taps_loaded, 16)
                def tile(i, t):
                    if i < B_TILES:
                        ve.wait_ge(in_done, ph.into + 2 * i + t + 1)
                        ve.tensor_scalar(b_rows[:, t, :], into[t][:, :], rstd[:, t:t + 1], None,
                                         ALU.mult).then_inc(in_read, 1)
                    else:
                        times(ph, i - B_TILES, t)

                for i in range(CONV_TILES):
                    nxt = ph.unit + IN_UNITS * (i + 1)
                    tile(i, 0)
                    if 0 < i <= B_TILES:
                        b_turned(i - 1, 1)
                    elif i > B_TILES:
                        z_turned(i - 1, 1)
                    lo_units(nxt, nxt + 2)
                    if i > B_TILES:
                        convolve(i - 1 - B_TILES)
                    else:
                        lo_units(nxt + 2, nxt + IN_UNITS)
                    tile(i, 1)
                    if i > B_TILES:
                        lo_units(nxt + 2, nxt + IN_UNITS)
                        product_lo(i - 1 - B_TILES)
                    b_turned(i, 0) if i < B_TILES else z_turned(i, 0)
                z_turned(CONV_TILES - 1, 1)
                convolve(CV_TILES - 1)
                lo_units(out0 + 4, out0 + 6)
                product_lo(CV_TILES - 1)
                lo_units(out0 + 6, out0 + KC)
                gates[0] += 2 * CV_TILES

            def pool_mixer(ph):
                ve.wait_ge(rel_turned, 1)
                ve.tensor_tensor(rel_rows, into[0][0:HEADS, 0:BAND], mask_rows,
                                 ALU.add).then_inc(rel_masked, 1)
                ve.wait_ge(pool_loaded, 48)
                link(ve.tensor_tensor(pool_rows[:, 0, :], pool_rows[:, 0, :], pool_rows[:, 1, :], ALU.mult))
                for t in range(HALVES):
                    step(ve.tensor_tensor(x[:, t, :], x[:, t, :], pool_rows[:, 0, :], ALU.add))
                for q in range(4):
                    turn_his[0] += 1
                    ve.wait_ge(turn_hi, turn_his[0])
                    chunks = slice(2 * q, 2 * q + 2)
                    ve.tensor_tensor(h_lo[:, :, chunks, :].rearrange("p t c k -> p c t k"),
                                     turn[q % 2][:, :].rearrange("p (c t k) -> p c t k", c=2, t=2),
                                     h_hi[:, :, chunks, :].rearrange("p t c k -> p c t k").bitcast(F32),
                                     ALU.subtract).then_inc(turn_read, 1)
                settle()

            def attn_mixer(ph):
                q0 = ph.unit + KV_UNITS
                out0 = q0 + 2 * IN_UNITS

                def cols_of(i):
                    return (slice(D, QKV), slice(D, D + P)) if i < 2 else \
                        (slice((i // 2 - 1) * 512, (i // 2) * 512),) * 2

                def heads_of(i):
                    return KV_HEADS if i < 2 else GROUP

                def item(i):
                    cols = cols_of(i)[0]
                    n = cols.stop - cols.start
                    ve.wait_ge(in_done, ph.into + in_at(TILE, i // 2, i % 2) + 1)
                    ve.scalar_tensor_tensor(out=qkv[:, i % 2, cols], in0=into[i % 2][:, 0:n],
                                            scalar=rstd[:, i % 2:i % 2 + 1], in1=bias_qkv[:, 0, cols],
                                            op0=ALU.mult, op1=ALU.add).then_inc(in_read, 1)

                def item_mean(i):
                    n = heads_of(i)
                    ve.wait_ge(squared, i + 1)
                    link(ve.tensor_reduce(qk_sum[:, i, 0:n],
                                          qk_sq[:, i % 2, 0:n * HD].rearrange("p (h d) -> p h d", d=HD),
                                          AX.X, ALU.add))
                    ve.tensor_scalar(qk_mean[:, i, 0:n], qk_sum[:, i, 0:n], EPS, None,
                                     ALU.add).then_inc(qk_mean_done, 1)

                def k_norm(t):
                    heads = qkv[:, t, D:D + P].rearrange("p (h d) -> p h d", d=HD)
                    ve.wait_ge(qk_rstd_done, t + 1)
                    k_rstd = qk_rstd[:, t, 0:KV_HEADS].unsqueeze(2).broadcast_to([P, KV_HEADS, HD])
                    link(ve.tensor_tensor(heads, heads, k_rstd, ALU.mult))
                    if t:
                        ve.wait_ge(turned, ph.fill + turn_at(ITEM, 0) + 1)
                    for a in range(2):
                        ins = ve.tensor_tensor(
                            k_twice.rearrange("p h (a d) -> p h a d", a=2)[:, :, a, :], heads,
                            qk_gain[:, 0, :].unsqueeze(1).broadcast_to([P, KV_HEADS, HD]), ALU.mult)
                        if a == 0:
                            step(ins)
                    ins.then_inc(k_ready, 1)

                def item_turned(i):
                    t, f = i % 2, ph.fill + turn_at(ITEM, i)
                    ve.wait_ge(turned, f + 1)
                    if i < 2:
                        to, chunks = k_t[:, :, t * P:(t + 1) * P], 2
                    else:
                        to, chunks = q_t[:, t, (i // 2 - 1) * 4:(i // 2) * 4, :], 4
                    ve.tensor_copy(to, bank(f % 2, chunks)).then_inc(turn_read, 1)

                def score_fills(g, t):
                    keys = (t + 1) * P
                    item = 2 + 2 * g + t
                    ve.wait_ge(qk_rstd_done, item + 1)
                    for b in range(GROUP // 2):
                        h = ph.into + in_at(SCORES, g, t) + b
                        ve.wait_ge(in_done, h + 1)
                        for m in range(2):
                            head = 4 * (b // 2) + 2 * m + b % 2
                            ins = ve.scalar_tensor_tensor(
                                out=scores[t][:, head, 0:keys], in0=into[h % 2][:, m * SEQ:m * SEQ + keys],
                                scalar=qk_rstd[:, item, head:head + 1],
                                in1=rel[:, g * GROUP + head, SEQ - keys:SEQ], op0=ALU.mult, op1=ALU.add)
                        ins.then_inc(in_read, 1)

                def maximum(g, t):
                    heads = slice(g * GROUP, (g + 1) * GROUP)
                    s = lambda k: soft[:, t, k, heads]
                    ve.wait_ge(in_read, ph.into + in_at(SCORES, g, t) + GROUP // 2)
                    link(ve.tensor_reduce(s(MAX), scores[t][:, :, 0:(t + 1) * P], AX.X, ALU.max))
                    link(ve.tensor_tensor(s(MAX), s(MAX), sink_row[:, heads], ALU.max))
                    link(ve.tensor_scalar(s(NEG_MAX), s(MAX), -1.0, None, ALU.mult))
                    ve.tensor_tensor(s(SINK), sink_row[:, heads], s(NEG_MAX), ALU.add).then_inc(max_done, 1)

                def probs_turned(g, t):
                    for n in range(2 * (t + 1)):
                        f = ph.fill + turn_at(PROBS, g, t) + n
                        a = prob_at(t) + 4 * n
                        ve.wait_ge(turned, f + 1)
                        ve.tensor_copy(probs_t[:, a:a + 4, :], bank(f % 2, 4)).then_inc(turn_read, 1)

                def output(g, t):
                    heads = slice(g * GROUP, (g + 1) * GROUP)
                    s = lambda k: soft[:, t, k, heads]
                    h = ph.into + in_at(VALUES, g, t)
                    ve.wait_ge(sink_done, 2 * g + t + 1)
                    ve.wait_ge(exp_done, GROUP * (2 * g + t + 1))
                    link(ve.tensor_tensor(s(DENOM), s(SUM), s(SINK_EXP), ALU.add))
                    link(ve.reciprocal(s(RECIP), s(DENOM)))
                    ve.wait_ge(in_done, h + 1)
                    ve.tensor_tensor(xn[:, t, g * 512:(g + 1) * 512].rearrange("p (h d) -> p h d", d=HD),
                                     into[h % 2][:, :].rearrange("p (h d) -> p h d", d=HD),
                                     s(RECIP).unsqueeze(2).broadcast_to([P, GROUP, HD]),
                                     ALU.mult).then_inc(in_read, 1)

                def output_split(g, t):
                    f = ph.fill + turn_at(OUTPUT, g, t)
                    turn_his[0] += 1
                    turn_split(f % 2, u_lo[:, t, 4 * g:4 * g + 4, :], u_hi[:, t, 4 * g:4 * g + 4, :],
                               turn_his[0])

                ve.wait_ge(attn_loaded, 16 * 5)
                link(ve.scalar_tensor_tensor(out=qk_gain[:, 0, :], in0=qk_gain[:, 0, :], scalar=HD ** -0.5,
                                             in1=qk_gain[:, 1, :], op0=ALU.mult, op1=ALU.mult))
                item(0)
                lo_units(q0 + 2, q0 + 3)
                item_mean(0)
                lo_units(q0 + 3, q0 + 4)
                item(1)
                k_norm(0)
                item_mean(1)
                lo_units(q0 + 4, q0 + 6)
                item(2)
                item_turned(0)
                k_norm(1)
                item_mean(2)
                lo_units(q0 + 6, q0 + 7)
                item(3)
                item_turned(1)
                item_turned(2)
                lo_units(q0 + 7, q0 + 8)
                item_mean(3)
                lo_units(out0, out0 + 2)
                item(4)
                item_turned(3)
                ve.wait_ge(rel_spread, 16)
                ve.wait_ge(bias_added, HALVES)
                score_fills(0, 0)
                score_fills(0, 1)
                maximum(0, 0)
                maximum(0, 1)
                item_turned(4)
                probs_turned(0, 0)
                item(5)
                item_mean(4)
                output(0, 0)
                ve.wait_ge(in_read, ph.into + in_at(TILE, 2, 1) + 1)
                probs_turned(0, 1)
                item_mean(5)
                item_turned(5)
                output_split(0, 0)
                lo_units(out0 + 2, out0 + 4)
                output(0, 1)
                score_fills(1, 0)
                output_split(0, 1)
                score_fills(1, 1)
                maximum(1, 0)
                maximum(1, 1)
                lo_units(out0 + 4, out0 + 6)
                probs_turned(1, 0)
                output(1, 0)
                probs_turned(1, 1)
                lo_units(out0 + 6, out0 + KC)
                output(1, 1)
                output_split(1, 0)
                output_split(1, 1)

            prev = None
            for ph in phases:
                boundary(prev, ph)
                {FFN: ffn, CONV: conv_mixer, POOL: pool_mixer, ATTN: attn_mixer}[ph.kind](ph)
                prev = ph
            for t in range(HALVES):
                for q in range(2):
                    residual(prev, t, q)


def _buckets():
    import math

    import numpy as np

    dist = 255 - np.arange(BAND)
    inside = (dist >= 0) & (dist < 128)
    n = np.where(inside, dist, 0)
    nf = np.maximum(n, 1).astype(np.float32)
    large = 16 + (np.log(nf / 16) / math.log(128 / 16) * 16).astype(np.int32)
    bucket = np.where(n < 16, n, np.minimum(large, 31)).astype(np.int32)
    onehot = np.zeros((32, BAND), np.float32)
    onehot[bucket[inside], np.nonzero(inside)[0]] = 1.0
    mask = np.where(inside, 0.0, -1e30).astype(np.float32)
    return onehot, np.ascontiguousarray(np.broadcast_to(mask, (HEADS, BAND)))


def _averaging():
    import numpy as np

    m = np.zeros((P, 4, 2, SEQ), np.float32)
    for g, win in enumerate(POOL_WINDOWS):
        for s in range(SEQ):
            for r in range(max(0, s - win + 1), s + 1):
                m[r % P, g, r // P, s] += np.float32(1.0 / min(s + 1, win))
            m[s % P, g, s // P, s] -= 1.0
    return m


def _stream(a):
    import numpy as np

    def wide(w, groups, tiles, width):
        w = w.reshape(-1, UNIT // (groups * width), P, groups, tiles, width)
        return w.transpose(4, 0, 2, 1, 3, 5).reshape(-1, P, UNIT)

    def ffn(w_in, w_out):
        a_in = wide(w_in, 2, FTILES, FT).reshape(FTILES, IN_UNITS, P, UNIT)
        a_out = w_out.reshape(FTILES, OUT_UNITS, P, UNIT)
        parts = [a_in[0]]
        for j in range(1, FTILES):
            parts += [a_in[j], a_out[j - 1]]
        return parts + [a_out[FTILES - 1]]

    def conv(w_in, w_out):
        return [wide(w_in[:, :D], 1, B_TILES, 512), wide(w_in[:, D:], 2, CV_TILES, FT),
                w_out.reshape(KC, P, UNIT)]

    def pool(w):
        return [w.reshape(2, 2, 2, P, FT).transpose(0, 3, 1, 2, 4).reshape(2, P, UNIT)]

    def attn(w_qkv, w_o):
        return [wide(w_qkv[:, D:], 1, 1, 256), wide(w_qkv[:, :D], 1, 2, 512), w_o.reshape(KC, P, UNIT)]

    parts = []
    for layer in range(DEPTH):
        parts += ffn(a["ffn1_w_in"][layer], a["ffn1_w_out"][layer])
        if layer % 3 == 0:
            parts += conv(a["conv_w_in"][layer // 3], a["conv_w_out"][layer // 3])
        elif layer % 3 == 1:
            parts += pool(a["pool_w"][0])
        else:
            parts += attn(a["attn_w_qkv"][0], a["attn_w_o"][0])
        parts += ffn(a["ffn2_w_in"][layer], a["ffn2_w_out"][layer])
    return np.concatenate(parts)


def kernel(**inputs):
    import concourse.bacc as bacc
    import numpy as np
    from concourse.bass_utils import run_bass_kernel_spmd

    a = {k: np.asarray(v) for k, v in inputs.items()}
    onehot, mask = _buckets()
    arrays = {
        "stream": _stream(a),
        "x_in": a["x"].reshape(SEQ, D),
        "gains": np.stack([a["ffn1_norm"], a["mix_norm"], a["ffn2_norm"]], 1).reshape(3 * DEPTH, D),
        "taps": a["conv_w"].reshape(2, TAPS, KC, P).transpose(3, 0, 1, 2),
        "pool_b": a["pool_b"][0],
        "pool_scale": a["pool_scale"][0],
        "b_qkv": a["attn_b_qkv"][0],
        "q_gain": a["attn_q_norm"][0],
        "k_gain": a["attn_k_norm"][0],
        "sinks": a["attn_sinks"][0],
        "b_o": a["attn_b_o"][0],
        "rel_bias": a["rel_bias"],
        "ident_in": np.eye(P, dtype=np.float32),
        "band_in": _averaging(),
        "onehot_in": onehot,
        "mask_in": mask,
    }
    arrays = {k: np.ascontiguousarray(v) for k, v in arrays.items()}
    nc = bacc.Bacc("TRN2", target_bir_lowering=False, num_devices=1)
    args = {k: nc.dram_tensor(k, v.shape, mybir.dt.from_np(v.dtype), kind="ExternalInput").ap()
            for k, v in arrays.items()}
    args["table"] = nc.dram_tensor("table", (HEADS, BAND), F32, kind="Internal").ap()
    args["spread"] = nc.dram_tensor("spread", (P, HEADS * SEQ), F32, kind="Internal").ap()
    args["out"] = nc.dram_tensor("y", (SEQ, D), F32, kind="ExternalOutput").ap()
    build(nc, **args)
    r = run_bass_kernel_spmd(nc, [arrays], core_ids=[0])
    return r.results[0]["y"].reshape(1, SEQ, D)
```
